# Optimizing a Trainium2 kernel written in Bass

```python
import jax, jax.numpy as jnp
from jax import lax
import numpy as np

D_MODEL = 1024
BATCH = 1
SEQ = 1024
DEPTH = 1

CONV_WIDTH = 1024
CONV_SIZE = 31
HEAD_DIM = 64
HEADS_PER_GROUP = 8
DILATION_GROUPS = ((128, 1), (512, 4), (2048, 16))
N_GROUPS = len(DILATION_GROUPS)
N_ATT_HEADS = N_GROUPS * HEADS_PER_GROUP
ATT_QKV = N_ATT_HEADS * HEAD_DIM
ATT_OUT = HEADS_PER_GROUP * HEAD_DIM
ROT_DIM = HEAD_DIM // 4
ROPE_THETA = 500000.0
BLOCK = 128
MAX_POS_OFFSET = 4096
EPS = 1e-6
NEG_INF = -1e30

IN_SPLITS = (CONV_WIDTH, CONV_WIDTH, CONV_WIDTH,
             ATT_QKV, ATT_QKV, ATT_QKV, ATT_OUT,
             D_MODEL, D_MODEL)
IN_COLS = sum(IN_SPLITS)


def _rmsnorm(x, g):
    xf = x.astype(jnp.float32)
    y = xf * lax.rsqrt(jnp.mean(xf * xf, axis=-1, keepdims=True) + EPS)
    return (y * g.astype(jnp.float32)).astype(x.dtype)

def _layernorm(x, g, b):
    xf = x.astype(jnp.float32)
    mu = jnp.mean(xf, axis=-1, keepdims=True)
    var = jnp.mean(jnp.square(xf - mu), axis=-1, keepdims=True)
    y = (xf - mu) * lax.rsqrt(var + EPS)
    return (y * g.astype(jnp.float32) + b.astype(jnp.float32)).astype(x.dtype)

def _partial_rope(t, positions):
    half = ROT_DIM // 2
    inv_freq = ROPE_THETA ** (-(jnp.arange(half, dtype=jnp.float32) * 2.0 / ROT_DIM))
    ang = positions.astype(jnp.float32)[..., None] * inv_freq
    cos = jnp.cos(ang)[:, :, None, :]
    sin = jnp.sin(ang)[:, :, None, :]
    tf = t.astype(jnp.float32)
    t1, t2 = tf[..., :half], tf[..., half:ROT_DIM]
    out = jnp.concatenate([t1 * cos - t2 * sin, t2 * cos + t1 * sin, tf[..., ROT_DIM:]], axis=-1)
    return out.astype(t.dtype)

def _dilated_window_group(q, k, v, window, dilation):
    b, s, h, e = q.shape
    L = s // dilation
    w_sub = window // dilation
    nb = -(-L // BLOCK)
    lp = nb * BLOCK

    def to_sub(t):
        return t.reshape(b, L, dilation, h, e).transpose(0, 2, 3, 1, 4)

    qs, ks, vs = to_sub(q), to_sub(k), to_sub(v)
    qs = jnp.pad(qs, ((0, 0), (0, 0), (0, 0), (0, lp - L), (0, 0)))
    ks = jnp.pad(ks, ((0, 0), (0, 0), (0, 0), (BLOCK, lp - L), (0, 0)))
    vs = jnp.pad(vs, ((0, 0), (0, 0), (0, 0), (BLOCK, lp - L), (0, 0)))
    qb = qs.reshape(b, dilation, h, nb, BLOCK, e)

    def band(t):
        prev = t[:, :, :, :lp].reshape(b, dilation, h, nb, BLOCK, e)
        cur = t[:, :, :, BLOCK:].reshape(b, dilation, h, nb, BLOCK, e)
        return jnp.concatenate([prev, cur], axis=-2)

    kb, vb = band(ks), band(vs)
    scores = jnp.einsum('bdhnqe,bdhnke->bdhnqk', qb.astype(jnp.float32),
                        kb.astype(jnp.float32)) * (e ** -0.5)
    qi = jnp.arange(BLOCK)[:, None]
    kj = jnp.arange(2 * BLOCK)[None, :]
    dist = qi + BLOCK - kj
    key_idx = jnp.arange(nb)[:, None, None] * BLOCK - BLOCK + kj[None]
    mask = (dist >= 0) & (dist <= w_sub) & (key_idx >= 0)
    scores = jnp.where(mask, scores, NEG_INF)
    m = jnp.max(scores, axis=-1)
    p = jnp.exp(scores - m[..., None])
    den = jnp.sum(p, axis=-1)
    o = jnp.einsum('bdhnqk,bdhnke->bdhnqe', p, vb.astype(jnp.float32)) / den[..., None]

    def from_sub(t):
        tail = t.shape[5:]
        t = t.reshape((b, dilation, h, lp) + tail)[:, :, :, :L]
        t = jnp.moveaxis(t, 3, 1)
        return t.reshape((b, s, h) + tail)

    return from_sub(o), from_sub(m), from_sub(den)

def first_inputs(seed: int = 0) -> dict:
    key = jax.random.key(seed)
    ks = jax.random.split(key, 16)
    f32 = jnp.float32
    x = jax.random.normal(ks[0], (BATCH, SEQ, D_MODEL), f32)
    c = jax.random.normal(ks[1], (BATCH, D_MODEL), f32)
    positions = (jnp.arange(SEQ, dtype=jnp.int32)[None, :]
                 + jax.random.randint(ks[2], (BATCH, 1), 0, MAX_POS_OFFSET, dtype=jnp.int32))
    norm_g = 1.0 + 0.05 * jax.random.normal(ks[3], (DEPTH, D_MODEL), f32)
    w_ada = 0.5 * D_MODEL ** -0.5 * jax.random.normal(ks[4], (DEPTH, D_MODEL, 3 * D_MODEL), f32)
    b_ada = 0.02 * jax.random.normal(ks[5], (DEPTH, 3 * D_MODEL), f32)
    w_in = D_MODEL ** -0.5 * jax.random.normal(ks[6], (DEPTH, D_MODEL, IN_COLS), f32)
    conv_w = CONV_SIZE ** -0.5 * jax.random.normal(ks[7], (DEPTH, CONV_SIZE, CONV_WIDTH), f32)
    conv_b = 0.02 * jax.random.normal(ks[8], (DEPTH, CONV_WIDTH), f32)
    conv_ln_g = 1.0 + 0.05 * jax.random.normal(ks[9], (DEPTH, CONV_WIDTH), f32)
    conv_ln_b = 0.02 * jax.random.normal(ks[10], (DEPTH, CONV_WIDTH), f32)
    w_conv_out = CONV_WIDTH ** -0.5 * jax.random.normal(ks[11], (DEPTH, CONV_WIDTH, D_MODEL), f32)
    w_att_out = ATT_OUT ** -0.5 * jax.random.normal(ks[12], (DEPTH, ATT_OUT, D_MODEL), f32)
    w_o = D_MODEL ** -0.5 * jax.random.normal(ks[13], (DEPTH, D_MODEL, D_MODEL), f32)
    final_g = 1.0 + 0.05 * jax.random.normal(ks[14], (D_MODEL,), f32)
    return {"x": x, "c": c, "positions": positions, "norm_g": norm_g,
            "w_ada": w_ada, "b_ada": b_ada, "w_in": w_in, "conv_w": conv_w,
            "conv_b": conv_b, "conv_ln_g": conv_ln_g, "conv_ln_b": conv_ln_b,
            "w_conv_out": w_conv_out, "w_att_out": w_att_out, "w_o": w_o,
            "final_g": final_g}

def first_block(x, c, positions, norm_g, w_ada, b_ada, w_in, conv_w, conv_b, conv_ln_g,
              conv_ln_b, w_conv_out, w_att_out, w_o, final_g):
    b, s, _ = x.shape
    split_idx = np.cumsum(IN_SPLITS)[:-1].tolist()
    for layer in range(DEPTH):
        mod = c @ w_ada[layer] + b_ada[layer]
        shift, scale, gate = [t[:, None, :] for t in jnp.split(mod, 3, axis=-1)]
        h = _rmsnorm(x, norm_g[layer]) * (1.0 + scale) + shift

        proj = h @ w_in[layer]
        (glu_a, glu_b, z_conv, q, k, v, z_att, g_conv, g_att) = jnp.split(proj, split_idx, axis=-1)

        u = glu_a * jax.nn.sigmoid(glu_b)
        u = lax.conv_general_dilated(
            u, conv_w[layer][:, None, :].astype(u.dtype), window_strides=(1,),
            padding=[(CONV_SIZE - 1, 0)], dimension_numbers=('NWC', 'WIO', 'NWC'),
            feature_group_count=CONV_WIDTH) + conv_b[layer]
        u = jax.nn.silu(_layernorm(u, conv_ln_g[layer], conv_ln_b[layer]))
        y_conv = (u * jax.nn.silu(z_conv)) @ w_conv_out[layer]

        q = _partial_rope(q.reshape(b, s, N_ATT_HEADS, HEAD_DIM), positions)
        k = _partial_rope(k.reshape(b, s, N_ATT_HEADS, HEAD_DIM), positions)
        v = v.reshape(b, s, N_ATT_HEADS, HEAD_DIM)
        outs, maxes, dens = [], [], []
        for gi, (window, dilation) in enumerate(DILATION_GROUPS):
            sl = slice(gi * HEADS_PER_GROUP, (gi + 1) * HEADS_PER_GROUP)
            o_g, m_g, d_g = _dilated_window_group(q[:, :, sl], k[:, :, sl], v[:, :, sl],
                                                  window, dilation)
            outs.append(o_g); maxes.append(m_g); dens.append(d_g)
        m_all = jnp.maximum(jnp.maximum(maxes[0], maxes[1]), maxes[2])
        wts = [d_g * jnp.exp(m_g - m_all) for m_g, d_g in zip(maxes, dens)]
        w_sum = wts[0] + wts[1] + wts[2]
        att = (wts[0][..., None] * outs[0] + wts[1][..., None] * outs[1]
               + wts[2][..., None] * outs[2]) / w_sum[..., None]
        att = att.reshape(b, s, ATT_OUT).astype(x.dtype)
        y_att = (att * jax.nn.silu(z_att)) @ w_att_out[layer]

        merged = jax.nn.sigmoid(g_conv) * y_conv + jax.nn.sigmoid(g_att) * y_att
        x = x + gate * (merged @ w_o[layer])
    return _rmsnorm(x, final_g)


POOL_WINDOWS = (2, 4, 8, 16)
N_POOL_GROUPS = len(POOL_WINDOWS)
POOL_WIDTH = D_MODEL // 2
POOL_GC = POOL_WIDTH // N_POOL_GROUPS
N_Q_HEADS = (D_MODEL // 2) // HEAD_DIM
N_KV_HEADS = 2
GROUP = N_Q_HEADS // N_KV_HEADS
ATTN_WIDTH = N_Q_HEADS * HEAD_DIM
KV_WIDTH = N_KV_HEADS * HEAD_DIM
WINDOW = 128
NEG_INF_2 = -1e30
ROT_DIM_2 = HEAD_DIM // 4
N_BRANCHES = 2
GATE_WIDTH = N_BRANCHES * D_MODEL
IN_SPLITS_2 = (POOL_WIDTH, POOL_WIDTH + ATTN_WIDTH, POOL_WIDTH + ATTN_WIDTH + KV_WIDTH,
             POOL_WIDTH + ATTN_WIDTH + 2 * KV_WIDTH)
IN_WIDTH = POOL_WIDTH + ATTN_WIDTH + 2 * KV_WIDTH + GATE_WIDTH
D_FF = 4 * D_MODEL


def _rmsnorm_2(x, g):
    xf = x.astype(jnp.float32)
    r = lax.rsqrt(jnp.mean(xf * xf, axis=-1, keepdims=True) + EPS)
    return (xf * r * g.astype(jnp.float32)).astype(x.dtype)

def _partial_rotary(t, cos, sin):
    half = ROT_DIM_2 // 2
    t1 = t[..., :half]
    t2 = t[..., half:ROT_DIM_2]
    c = cos[None, :, None, :].astype(t.dtype)
    s = sin[None, :, None, :].astype(t.dtype)
    return jnp.concatenate([t1 * c - t2 * s, t2 * c + t1 * s, t[..., ROT_DIM_2:]], axis=-1)

def _multiscale_pool(u, w_pool, pool_scale):
    B, S, _ = u.shape
    uf = u.astype(jnp.float32)
    cs = jnp.pad(jnp.cumsum(uf, axis=1), ((0, 0), (1, 0), (0, 0)))
    t = jnp.arange(S)
    pooled = []
    for gi, w in enumerate(POOL_WINDOWS):
        c = cs[..., gi * POOL_GC:(gi + 1) * POOL_GC]
        upper = c[:, 1:]
        lower = jnp.pad(c[:, :S + 1 - w], ((0, 0), (w - 1, 0), (0, 0)))
        count = jnp.minimum(t + 1, w).astype(jnp.float32)[None, :, None]
        pooled.append((upper - lower) / count)
    pooled = jnp.stack(pooled, axis=2)
    diff = (pooled - uf.reshape(B, S, N_POOL_GROUPS, POOL_GC)).astype(u.dtype)
    mixed = jnp.einsum('bsgc,gcd->bsgd', diff, w_pool)
    return mixed.reshape(B, S, POOL_WIDTH) * pool_scale

def _sliding_window_sink_attention(q, k, v, sinks):
    B, S = q.shape[0], q.shape[1]
    nb = S // BLOCK
    qb = q.reshape(B, nb, BLOCK, N_KV_HEADS, GROUP, HEAD_DIM)

    def with_prev(t):
        tb = t.reshape(B, nb, BLOCK, N_KV_HEADS, HEAD_DIM)
        prev = jnp.pad(tb[:, :-1], ((0, 0), (1, 0), (0, 0), (0, 0), (0, 0)))
        return jnp.concatenate([prev, tb], axis=2)

    kk = with_prev(k)
    vv = with_prev(v)
    scale = HEAD_DIM ** -0.5
    s = jnp.einsum('bnqhgd,bnkhd->bnhgqk', qb, kk).astype(jnp.float32) * scale
    qi = jnp.arange(BLOCK)[:, None]
    kj = jnp.arange(2 * BLOCK)[None, :]
    rel = qi + BLOCK - kj
    band = (rel >= 0) & (rel < WINDOW)
    has_prev = (jnp.arange(nb) > 0)[:, None, None] | (kj >= BLOCK)[None]
    valid = band[None] & has_prev
    s = jnp.where(valid[None, :, None, None], s, NEG_INF_2)
    sink = jnp.broadcast_to(sinks.astype(jnp.float32).reshape(1, 1, N_KV_HEADS, GROUP, 1, 1),
                            s.shape[:-1] + (1,))
    p = jax.nn.softmax(jnp.concatenate([s, sink], axis=-1), axis=-1)[..., :-1]
    o = jnp.einsum('bnhgqk,bnkhd->bnqhgd', p.astype(v.dtype), vv)
    return o.reshape(B, S, ATTN_WIDTH)

def second_inputs(seed: int = 0) -> dict:
    key = jax.random.key(seed)
    ks = jax.random.split(key, 16)
    nrm = jax.random.normal
    f32 = jnp.float32

    def gain(k):
        return 1.0 + 0.1 * nrm(k, (DEPTH, D_MODEL), f32)

    return {
        "x": nrm(ks[0], (BATCH, SEQ, D_MODEL), f32),
        "g_mix_pre": gain(ks[1]),
        "w_in": nrm(ks[2], (DEPTH, D_MODEL, IN_WIDTH), f32) * D_MODEL ** -0.5,
        "b_in": 0.02 * nrm(ks[3], (DEPTH, IN_WIDTH), f32),
        "w_pool": nrm(ks[4], (DEPTH, N_POOL_GROUPS, POOL_GC, POOL_GC), f32) * POOL_GC ** -0.5,
        "pool_scale": 1.0 + 0.1 * nrm(ks[5], (DEPTH, POOL_WIDTH), f32),
        "attn_sinks": 0.5 * nrm(ks[6], (DEPTH, N_Q_HEADS), f32),
        "w_branch_pool": nrm(ks[7], (DEPTH, POOL_WIDTH, D_MODEL), f32) * POOL_WIDTH ** -0.5,
        "w_branch_attn": nrm(ks[8], (DEPTH, ATTN_WIDTH, D_MODEL), f32) * ATTN_WIDTH ** -0.5,
        "w_out": nrm(ks[9], (DEPTH, D_MODEL, D_MODEL), f32) * D_MODEL ** -0.5,
        "g_mix_post": gain(ks[10]),
        "g_mlp_pre": gain(ks[11]),
        "w_up": nrm(ks[12], (DEPTH, D_MODEL, D_FF), f32) * D_MODEL ** -0.5,
        "w_down": nrm(ks[13], (DEPTH, D_FF, D_MODEL), f32) * D_FF ** -0.5,
        "g_mlp_post": gain(ks[14]),
    }

def second_block(x, g_mix_pre, w_in, b_in, w_pool, pool_scale, attn_sinks, w_branch_pool,
              w_branch_attn, w_out, g_mix_post, g_mlp_pre, w_up, w_down, g_mlp_post):
    B, S, _ = x.shape
    pos = jnp.arange(S, dtype=jnp.float32)
    inv_freq = ROPE_THETA ** (-jnp.arange(0, ROT_DIM_2, 2, dtype=jnp.float32) / ROT_DIM_2)
    ang = pos[:, None] * inv_freq[None, :]
    cos, sin = jnp.cos(ang), jnp.sin(ang)

    for l in range(DEPTH):
        h = _rmsnorm_2(x, g_mix_pre[l])
        proj = jnp.einsum('bsd,de->bse', h, w_in[l]) + b_in[l]
        u_pool, q, k, v, gates = jnp.split(proj, IN_SPLITS_2, axis=-1)

        y_pool = _multiscale_pool(u_pool, w_pool[l], pool_scale[l])

        q = _partial_rotary(q.reshape(B, S, N_Q_HEADS, HEAD_DIM), cos, sin)
        k = _partial_rotary(k.reshape(B, S, N_KV_HEADS, HEAD_DIM), cos, sin)
        v = v.reshape(B, S, N_KV_HEADS, HEAD_DIM)
        y_attn = _sliding_window_sink_attention(
            q.reshape(B, S, N_KV_HEADS, GROUP, HEAD_DIM), k, v, attn_sinks[l])

        g = jax.nn.sigmoid(gates.astype(jnp.float32)).astype(x.dtype)
        g_pool, g_attn = g[..., :D_MODEL], g[..., D_MODEL:]
        merged = (g_pool * jnp.einsum('bsc,cd->bsd', y_pool, w_branch_pool[l])
                  + g_attn * jnp.einsum('bsc,cd->bsd', y_attn, w_branch_attn[l]))
        mix = jnp.einsum('bsd,de->bse', merged, w_out[l])
        x = x + _rmsnorm_2(mix, g_mix_post[l])

        h2 = _rmsnorm_2(x, g_mlp_pre[l])
        ff = jnp.einsum('bsf,fd->bsd',
                        jnp.square(jax.nn.relu(jnp.einsum('bsd,df->bsf', h2, w_up[l]))), w_down[l])
        x = x + _rmsnorm_2(ff, g_mlp_post[l])
    return x


def setup_inputs(seed=0):
    out = dict(first_inputs(seed))
    for name, value in second_inputs(seed + 1).items():
        if name != "x":
            out[name + "_2"] = value
    return out


def reference(
    x, c, positions, norm_g, w_ada, b_ada, w_in, conv_w, conv_b, conv_ln_g, conv_ln_b,
    w_conv_out, w_att_out, w_o, final_g, g_mix_pre_2, w_in_2, b_in_2, w_pool_2, pool_scale_2,
    attn_sinks_2, w_branch_pool_2, w_branch_attn_2, w_out_2, g_mix_post_2, g_mlp_pre_2, w_up_2,
    w_down_2, g_mlp_post_2,
):
    x = first_block(
        x, c, positions, norm_g, w_ada, b_ada, w_in, conv_w, conv_b, conv_ln_g, conv_ln_b,
        w_conv_out, w_att_out, w_o, final_g,
    )
    return second_block(
        x, g_mix_pre_2, w_in_2, b_in_2, w_pool_2, pool_scale_2, attn_sinks_2, w_branch_pool_2,
        w_branch_attn_2, w_out_2, g_mix_post_2, g_mlp_pre_2, w_up_2, w_down_2, g_mlp_post_2,
    )


_drawn_inputs = setup_inputs


def setup_inputs(seed=0):
    import zlib

    import numpy as np

    out = dict(_drawn_inputs(seed))
    spreads = {}
    factors = {'norm_g': 4.536,
     'b_ada': 5.647,
     'conv_b': 8.0,
     'conv_ln_g': 6.736,
     'conv_ln_b': 25.438,
     'b_in_2': 3.113,
     'attn_sinks_2': 8.0}
    for name, (base, spread) in spreads.items():
        noise = np.random.default_rng([zlib.crc32(name.encode()), seed]).standard_normal(out[name].shape)
        drawn = base * np.exp(spread * noise) if base else spread * noise
        out[name] = __import__('jax').numpy.asarray(drawn.astype(out[name].dtype))
    for name, factor in factors.items():
        out[name] = (out[name] * factor).astype(out[name].dtype)
    return out
```

```python
from contextlib import ExitStack

import numpy as np
import concourse.bass as bass
from concourse import mybir

F32 = mybir.dt.float32
F32R = mybir.dt.float32r
I32 = mybir.dt.int32
ALU = mybir.AluOpType
ACT = mybir.ActivationFunctionType

P = 128
S = 1024
D = 1024
NB = S // P
KT = D // P
HALF = 512
HD = 64
HPG = 8
NG = 3
TAPS = 31
DFF = 4 * D
FC = 256
EPS = 1e-6
NEG = -1e30
QKV0, ZATT0, GATE0 = 3072, 7680, 8192
THETA = 500000.0
POOL_W = (2, 4, 8, 16)
ACC = 4
RAW = 4
EVN = 3


def plan():
    chunks, units, items, last = [], [], [], {}

    def chunk(key, us):
        chunks.append(key)
        units.extend(us)
        last[len(chunks) - 1] = [u for u in us if u[0] not in ("qt", "kt")][-1]

    def f_units(name, tiles):
        return [(name, t, h) for t in tiles for h in range(2)]

    def t_units(name, cols):
        return [(name, B, cols) for B in range(NB)]

    units += [("xt", B, h) for B in range(NB) for h in range(2)]

    def qkv(g, lots):
        late = []
        for t in lots:
            us = []
            for B in range(NB):
                us.append((t, g, B))
                us += late
                late = [(t + "t", g, B)] if t in "qk" else []
                if t in "qk":
                    items.append(("rope", (t, g, B)))
            if t == lots[-1]:
                us += late
            chunk((t, g), us)

    def glu(j):
        us = []
        for t in (2 * j, 2 * j + 1):
            for h in range(2):
                us += [("ub", t, h), ("ua", t, h)]
                items.append(("store", ("ua", t, h)))
        chunk(("glu", j), us)

    def stored(name, j):
        us = f_units(name, range(4 * j, 4 * j + 4))
        items.extend(("store", u) for u in us)
        chunk((name, j), us)

    qkv(0, "qkv")
    for j in range(3):
        glu(j)
    qkv(1, "qkv")
    glu(3), stored("gc", 0), stored("gc", 1)
    qkv(2, "qkv")
    stored("ga", 0), stored("ga", 1), stored("za", 0)
    for j in range(2):
        us = []
        for i, u in enumerate(f_units("zc", range(4 * j, 4 * j + 4))):
            B = 4 * j + i // 2
            us += [("ct", B, 0), ("ct", B, 1), u] if i % 2 == 0 else [("lt", B, 0), ("lt", B, 1), u, ("at", B, 0)]
            items.append(("store", u))
        chunks.append(("zc", j))
        units.extend(us)
        last[len(chunks) - 1] = [u for u in us if u[0] == "zc"][-1]
    for j in range(2):
        chunk(("yc", j), f_units("yc", range(4 * j, 4 * j + 4)))
    chunk(("ya", 0), f_units("ya", range(8)))
    chunk(("wo", 0), t_units("wo", 0))
    chunk(("wo", 1), t_units("wo", 1))
    units.extend(("ht", B, h) for B in range(NB) for h in range(2))
    chunk(("pl", 0), f_units("pl", range(4)))
    qkv(3, "q")
    us = [("kv", 3, 0)]
    for B in range(1, NB):
        us += [("kv", 3, B), ("kt", 3, B - 1)]
    chunk(("kv", 3), us + [("kt", 3, NB - 1)])
    items.extend(("rope", ("k", 3, B)) for B in range(NB))
    units.extend(("pm", t, h) for t in range(4) for h in range(2))
    for name in ("g2p", "g2a"):
        stored(name, 0), stored(name, 1)
    units.extend(("a2", B, 0) for B in range(NB))
    chunk(("yp", 0), f_units("yp", range(8)))
    chunk(("yb", 0), f_units("yb", range(8)))
    chunk(("w2", 0), t_units("w2", 0))
    chunk(("w2", 1), t_units("w2", 1))
    units.extend(("mt", B, h) for B in range(NB) for h in range(2))
    U = {u: n for n, u in enumerate(units)}
    assert len(U) == len(units)
    return chunks, units, items, U, last


def att_share(C):
    return C * 8 * 24 // 64


def units_done(C, s):
    per = att_share(C)
    return range((s * per) // 24, ((s + 1) * per) // 24)


def tap_plan():
    todo, at = {}, 0

    def give(keys, n):
        nonlocal at
        for u in keys:
            m = min(n, 16 * TAPS - at)
            todo[u] = (at, at + m)
            at += m

    give([("step", 0, s) for s in range(26, 64)], 1)
    give([(t, 1, B) for t in "qkv" for B in range(NB)], 5)
    give([("step", 1, s) for s in range(64)], 2)
    give([(t, 2, B) for t in "qkv" for B in range(NB)], 4)
    give([("step", 2, s) for s in range(64)], 2)
    assert at == 16 * TAPS, at
    return todo


def build(nc, A, out):
    chunks, units, items, U, chunk_last = plan()
    taps_after = tap_plan()
    M0 = len(units)
    assert M0 % ACC == 0
    M4 = M0 // ACC
    E = {key: n for n, (kind, key) in enumerate(items)}
    chunk_of = {}
    for c, key in enumerate(chunks):
        chunk_of[key] = c

    with ExitStack() as ctx:
        def sb(name, cols, dt=F32):
            return ctx.enter_context(nc.sbuf_tensor(name, [P] + list(cols), dt))

        def sem(name):
            return ctx.enter_context(nc.semaphore(name))

        def dram(name, shape):
            return nc.dram_tensor(name, shape, F32, kind="Internal").ap()

        act_hi = sb("act_hi", [KT, S], F32R)
        act_lo = sb("act_lo", [KT, S], F32R)
        w_hi = sb("w_hi", [2, KT, HALF], F32R)
        w_lo = sb("w_lo", [2, KT, HALF], F32R)
        raw = sb("raw", [RAW, HALF])
        big = sb("big", [8 * S])
        vreg = sb("vreg", [4 * S])
        scr = sb("scr", [4668])
        ident = sb("ident", [P])
        band = sb("band", [2 * P])
        resid = sb("resid", [P])
        cosT = sb("cosT", [4 * NB, 8])
        sinT = sb("sinT", [4 * NB, 8])
        col = sb("col", [96])
        stat = sb("stat", [NB, 16])
        small = sb("small", [182])
        ps = [ctx.enter_context(nc.psum_tensor(f"ps{i}", [P, HALF], F32)) for i in range(8)]
        acc, ps_s = [t[:, :] for t in ps[:ACC]], [t[:, :] for t in ps[4:6]]
        ps_t, ps_o = ps[6][:, :], ps[7][:, :]

        mod_d = dram("mod_d", [1, 3 * D])
        u_d, c_d = dram("u_d", [D, S]), dram("c_d", [D, S])
        gate_d = {n: dram(n + "_d", [D, S]) for n in ("gc", "ga", "zc", "g2p", "g2a")}
        gate_d["za"] = dram("za_d", [HALF, S])
        o_d, st_d = dram("o_d", [NG, S, HALF]), dram("st_d", [NG, S, 16])
        x1_d, x2_d = dram("x1_d", [S, D]), dram("x2_d", [S, D])
        yp_d = dram("yp_d", [HALF, S])

        featT = big[:, :].rearrange("p (k s) -> p k s", k=KT)
        tokT = big[:, :].rearrange("p (b d) -> p b d", b=NB)
        qT = big[:, 0:4 * S].rearrange("p (h s) -> p h s", h=4)
        kT = big[:, 4 * S:8 * S].rearrange("p (h s) -> p h s", h=4)
        V = vreg[:, :].rearrange("p (b c) -> p b c", b=NB)
        kT2 = big[:, 4 * S:5 * S]
        V2 = big[:, 5 * S:6 * S].rearrange("p (b c) -> p b c", b=NB)
        bq_bc = big[:, 6 * S:6 * S + 512]
        bkv_bc = big[:, 6 * S + 512:6 * S + 768]
        wpool = big[:, 6 * S + 768:6 * S + 1280].rearrange("p (g d) -> p g d", g=4)
        attzT = vreg[:, :].rearrange("p (k s) -> p k s", k=4)
        prob = [scr[:, i * 256:(i + 1) * 256] for i in range(2)]
        probT = [scr[:, 512 + i * 256:512 + (i + 1) * 256] for i in range(2)]
        obuf = [scr[:, 1024 + i * 256:1024 + (i + 1) * 256] for i in range(2)]
        ev = [scr[:, 1536 + i * HALF:1536 + (i + 1) * HALF] for i in range(EVN)]
        cu = [scr[:, 3072 + i * 542:3072 + (i + 1) * 542] for i in range(2)]
        ca = scr[:, 4156:4156 + HALF]
        bada = scr[0:6, 2048:2048 + HALF]
        mrow = [scr[0:1, 3104 + i * HALF:3104 + (i + 1) * HALF] for i in range(3)]
        xs = [scr[:, i * S:(i + 1) * S] for i in range(2)]
        cw = [small[:, 80 + i * TAPS:80 + (i + 1) * TAPS] for i in range(2)]
        ada = vreg[:, :].rearrange("p (i n) -> p i n", i=8)

        c_ng, c_gs, c_sh = col[:, 0:8], col[:, 8:16], col[:, 16:24]
        c_cb, c_lg, c_lb = col[:, 24:32], col[:, 32:40], col[:, 40:48]
        c_lgh, c_lbh = col[:, 48:56], col[:, 56:64]
        c_gb = col[:, 64:80]
        c_ps, c_pb = col[:, 80:84], col[:, 84:88]
        c_ns = col[:, 88:96]

        tiny = small[:, 142:182]
        posi = scr[:, 2560:2592].bitcast(I32)
        cb = scr[:, 0:S]
        un = cb
        zab = scr[:, S:S + HALF]
        og = [scr[:, 3072 + HALF * g:3072 + HALF * (g + 1)] for g in range(NG)]
        og_all = scr[:, 3072:3072 + NG * HALF].rearrange("p (g c) -> p g c", g=NG)
        sg = small[:, 8:56].rearrange("p (g c) -> p g c", g=NG)
        tt = [scr[:, i * S:(i + 1) * S] for i in range(2)]
        zt = [scr[:, 2048:3072], scr[:, 3072:4096]]
        gt = [scr[:, i * HALF:(i + 1) * HALF] for i in range(4)]
        gtmp = [scr[:, 2048 + i * HALF:2048 + (i + 1) * HALF] for i in range(2)]
        bc = [[vreg[:, i * S:(i + 1) * S] for i in range(3)] for _ in range(3)]
        xn = [vreg[:, 3 * S:4 * S], scr[:, 3072:4096]]
        junk = scr[:, 2048:3072]
        xt2 = [scr[:, i * HALF:(i + 1) * HALF] for i in range(2)]
        res = [scr[:, i * S:(i + 1) * S] for i in range(2)]
        yv = vreg[:, :].rearrange("p (b c) -> p b c", b=NB)
        relu = [scr[:, i * HALF:(i + 1) * HALF] for i in range(4)]
        sq = [scr[:, 2048 + i * HALF:2048 + (i + 1) * HALF] for i in range(4)]
        epsc = tiny[:, 38:40]
        posf, ang = scr[:, 2592:2624], scr[:, 2624:2880]
        angr = ang.rearrange("p (a j) -> p a j", j=8)
        angs, angc, turns = (scr[:, i * 256:(i + 1) * 256] for i in range(3))
        rx, ry = scr[:, 0:128], scr[:, 128:256]
        pw = [scr[:, 256:1280], scr[:, 3072:4096]]
        flat = stat[:, :, :].rearrange("p b c -> p (b c)")

        parity = cosT[:, 0:16, :].rearrange("p a j -> p (a j)").bitcast(I32)
        POOL_CONSTS = 2 + 3 + 15 + 1

        acc_ready = sem("acc_ready")
        acc_free = [sem(f"acc_free{i}") for i in range(ACC)]
        raw_ld = [sem(f"raw_ld{i}") for i in range(RAW)]
        w_hi_done, w_ready = sem("w_hi_done"), sem("w_ready")
        hi_done, lo_done = sem("hi_done"), sem("lo_done")
        ev_st = [sem(f"ev_st{i}") for i in range(EVN)]
        tanh_done = sem("tanh_done")
        roped = sem("roped")
        scores, att_max, probs = sem("scores"), sem("att_max"), sem("probs")
        probs_t, pt_out, pv, o_out = sem("probs_t"), sem("pt_out"), sem("pv"), sem("o_out")
        ob_st = [sem("ob_st0"), sem("ob_st1")]
        dve_step, act_step, pool_step = sem("dve_step"), sem("act_step"), sem("pool_step")
        const_ld, pos_ld, consts = sem("const_ld"), sem("pos_ld"), sem("consts")
        x_ld = [sem("x_ld0"), sem("x_ld1")]
        x_sq, x_norm = sem("x_sq"), sem("x_norm")
        ada_ld = [sem(f"ada_ld{i}") for i in range(8)]
        ada_used, ada_row, ada_col = sem("ada_used"), sem("ada_row"), sem("ada_col")
        mod_st = [sem(f"mod_st{i}") for i in range(3)]
        gs_ready, h_aff = sem("gs_ready"), sem("h_aff")
        ang_ready, rope_tab = sem("ang_ready"), sem("rope_tab")
        u_ld = [sem("u_ld0"), sem("u_ld1")]
        tap, c_st, pad0 = sem("tap"), sem("c_st"), sem("pad0")
        stat_st, stat_free = sem("stat_st"), sem("stat_free")
        cb_ld, ln_var, ln_sd, ln_rs, ln_un = (sem(n) for n in ("cb_ld", "ln_var", "ln_sd", "ln_rs", "ln_un"))
        o_ld, cmb_m, cmb_e, att_done, za_ld = (sem(n) for n in ("o_ld", "cmb_m", "cmb_e", "att_done", "za_ld"))
        z_ld, uz_t, uz_w = [sem("z_ld0"), sem("z_ld1")], sem("uz_t"), sem("uz_w")
        g_ld = [sem(f"g_ld{i}") for i in range(4)]
        mrg = sem("mrg")
        bc_ld = sem("bc_ld")
        n_ld = [[sem(f"n{r}_ld{i}") for i in range(2)] for r in range(3)]
        n_x, n_s1, n_y, n_s2, n_xn, n_st = ([sem(f"n{r}_{t}") for r in range(3)]
                                            for t in ("x", "s1", "y", "s2", "xn", "st"))
        p_in, p_diff, yp_st, yp_ld, y2_den, y2_done = (sem(n) for n in ("p_in", "p_diff", "yp_st", "yp_ld",
                                                                        "y2_den", "y2_done"))
        rel, out_st = sem("rel"), sem("out_st")
        piece_seen = sem("piece_seen")
        c_ld, eps_ready, v2_out, y2_exp = sem("c_ld"), sem("eps_ready"), sem("v2_out"), sem("y2_exp")

        splits = ([("h", k) for k in range(8)] + [("uz", k) for k in range(8)] + [("az", k) for k in range(4)]
                  + [("mg", k) for k in range(8)] + [("ht", i) for i in range(16)]
                  + [("a2", B) for B in range(8)] + [("y2", k) for k in range(4)]
                  + [("m2", k) for k in range(8)] + [("mt", i) for i in range(16)])
        SPLIT = {key: n + 1 for n, key in enumerate(splits)}
        SPLIT_LO = {key: n + 1 for n, key in enumerate(k for k in splits if k[0] not in ("ht", "a2", "mt"))}
        TANH = {u: n + 1 for n, u in enumerate([u for u in units if u[0] in ("za", "zc")])}
        ROPE = {key: n + 1 for n, key in enumerate(k for kind, k in items if kind == "rope")}

        def wait_unit(eng, u):
            eng.wait_ge(acc_ready, U[u] + 1)

        def wait_evac(eng, u):
            eng.wait_ge(acc_free[U[u] % ACC], U[u] // ACC + 1)

        def bank(u):
            return acc[U[u] % ACC]

        def free_of(u):
            return acc_free[U[u] % ACC]

        def stores_in_slot(e):
            return sum(1 for n in range(e % EVN, e + 1, EVN) if items[n][0] == "store")

        def wait_stored(eng, key):
            eng.wait_ge(ev_st[E[key] % EVN], 16 * stores_in_slot(E[key]))

        def wait_slot(eng, key):
            e = E[key] - EVN
            if e >= 0:
                kind, old = items[e]
                if kind == "store":
                    eng.wait_ge(ev_st[e % EVN], 16 * stores_in_slot(e))
                else:
                    wait_unit(eng, (old[0] + "t",) + old[1:])

        def slot(key):
            return ev[E[key] % EVN]

        GATED = [(n, t, h) for n in ("yc", "ya", "yp", "yb") for t in range(8) for h in range(2)]

        def ob_count(quad):
            return 16 * len(range(quad % 2, quad, 2))

        OB_TOTAL = [ob_count(48), ob_count(49)]

        def att_cfg(g, B):
            prev = {0: B > 0, 1: B % 2 == 1, 2: False, 3: B > 0}[g]
            if prev:
                return (B - 1) * P, 2 * P, band[:, :]
            return B * P, P, (resid[:, :] if g == 2 else band[:, P:2 * P])

        ATT_STAGES = {0: [("glu", j) for j in range(3)], 1: [("glu", 3), ("gc", 0), ("gc", 1)],
                      2: [("ga", 0), ("ga", 1), ("za", 0)], 3: [(n, j) for n in ("g2p", "g2a") for j in range(2)]}

        def chunk_units(key):
            c = chunk_of[key]
            n = U[chunk_last[c]]
            return units[n - 7:n + 1]

        def att_units(g):
            return [u for key in ATT_STAGES[g] for u in chunk_units(key)]

        def unit_range(first, last):
            return units[U[first]:U[last] + 1]

        STAGE_QKV = {g: unit_range(("q", g, 0), ("v", g, 7)) for g in range(NG)}
        STAGE_Z = unit_range(("ct", 0, 0), ("at", 7, 0))

        w_in, w_in2 = A["w_in"][0], A["w_in_2"][0]

        def piece_src(key, s):
            name, j = key
            rows = slice(P * s, P * s + P)
            whole = slice(0, HALF)
            if name in "qkv" and j < NG:
                c0 = QKV0 + 1536 * "qkv".index(name) + HALF * j
                return [(whole, w_in[rows, c0:c0 + HALF])]
            if name == "glu":
                return [(slice(0, 256), w_in[rows, 256 * j:256 * j + 256]),
                        (slice(256, 512), w_in[rows, D + 256 * j:D + 256 * j + 256])]
            if name in ("gc", "ga", "zc", "za"):
                c0 = {"gc": GATE0, "ga": GATE0 + D, "zc": 2 * D, "za": ZATT0}[name] + HALF * j
                return [(whole, w_in[rows, c0:c0 + HALF])]
            if name in ("pl", "q", "kv", "g2p", "g2a"):
                c0 = {"pl": 0, "q": 512, "kv": 1024, "g2p": 1280, "g2a": 2304}[name]
                if name in ("g2p", "g2a"):
                    c0 += HALF * j
                n = 256 if name == "kv" else HALF
                return [(slice(0, n), w_in2[rows, c0:c0 + n])]
            if name in ("yc", "wo", "w2"):
                w = A[{"yc": "w_conv_out", "wo": "w_o", "w2": "w_out_2"}[name]][0]
                return [(whole, w[rows, HALF * j:HALF * j + HALF])]
            w = A[{"ya": "w_att_out", "yp": "w_branch_pool_2", "yb": "w_branch_attn_2"}[name]][0]
            return [(whole, w[P * (s // 2):P * (s // 2) + P, HALF * (s % 2):HALF * (s % 2) + HALF])]

        PIECES = [(c, s) for c in range(len(chunks)) for s in range(8)]
        raw_total = {}
        count = [0] * RAW
        for n, (c, s) in enumerate(PIECES):
            count[n % RAW] += 16 * len(piece_src(chunks[c], s))
            raw_total[n] = count[n % RAW]
        RAW_BASE = list(count)
        NP0 = len(PIECES)

        w_up, w_down = A["w_up_2"][0], A["w_down_2"][0]

        def up_src(j, p):
            return w_up.rearrange("(a k p) n -> a p k n", k=2, p=P)[p][:, :, bass.ds(j * FC, FC)]

        def down_src(j, p):
            return w_down[bass.ds(j * FC + P * (p // 2), P), HALF * (p % 2):HALF * (p % 2) + HALF]

        up_w = [w[:, 0, 0:4, :].rearrange("p a n -> p (a n)").rearrange("p (k n) -> p k n", k=KT)
                for w in (w_hi, w_lo)]
        down_w = [w[:, 0, 4:8, :].rearrange("p a n -> p (a n)").rearrange("p (k n) -> p k n", k=2)
                  for w in (w_hi, w_lo)]
        hid = [w[:, 1, :, :].rearrange("p a n -> p (a n)").rearrange("p (i t s) -> p i t s", i=2, t=2)
               for w in (w_hi, w_lo)]
        NJ = DFF // FC

        def up_unit(j):
            return M0 + 20 * j - 16

        def down_unit(j):
            return M0 + 20 * j + 8

        MLP_LAST = M0 + 4 * NJ + 16 * NJ

        block = ctx.enter_context(nc.Block())

        PROJ = {"q", "k", "v", "kv", "ua", "ub", "gc", "ga", "za", "zc", "yc", "ya", "wo", "pl", "g2p", "g2a",
                "yp", "yb", "w2"}
        unit_chunk = {}
        for c, key in enumerate(chunks):
            n1 = U[chunk_last[c]] + 1
            n0 = U[chunk_last[c - 1]] + 1 if c else 0
            for i, u in enumerate([u for u in units[n0:n1] if u[0] in PROJ]):
                unit_chunk[u] = (c, i)

        def token_block(g, B):
            if g == 1:
                return lambda t: t[:, HALF * (B % 2) + B // 2:HALF * (B % 2) + HALF:4]
            if g == 2:
                return lambda t: t[:, B::8]
            return lambda t: t[:, B * P:(B + 1) * P]

        @block.sync
        def _(sp):
            piece = [0]

            def next_piece():
                n = piece[0]
                if n >= NP0:
                    return
                if n >= RAW:
                    sp.wait_ge(w_ready, n - RAW + 1)
                c, s = PIECES[n]
                for cols, src in piece_src(chunks[c], s):
                    sp.dma_start(raw[:, n % RAW, cols], src).then_inc(raw_ld[n % RAW], 16)
                piece[0] += 1

            def prefetch(u):
                if u in unit_chunk:
                    c, i = unit_chunk[u]
                    if i < 8 and piece[0] < 8 * (c + 1) + i + 1:
                        next_piece()

            def store_item(u, dst):
                wait_evac(sp, u)
                sp.dma_start(dst, slot(u)).then_inc(ev_st[E[u] % EVN], 16)

            def feature_tile(d, t, h):
                return d[P * t:P * t + P, HALF * h:HALF * h + HALF]

            def cols_of(v):
                return v.rearrange("(k p) -> p k", p=P)

            for B in range(2):
                sp.dma_start(xs[B], A["x"][0, P * B:P * B + P, :]).then_inc(x_ld[B], 16)
            sp.dma_start(small[:, 0:8], A["c"]).then_inc(c_ld, 16)
            sp.dma_start(bada, A["b_ada"][0].rearrange("(n c) -> n c", n=6)).then_inc(c_ld, 16)

            def ada_piece(p):
                n, k = p // 8, p % 8
                if p >= 8:
                    sp.wait_ge(ada_used, p - 7)
                sp.dma_start(ada[:, k, :], A["w_ada"][0, P * k:P * k + P, HALF * n:HALF * n + HALF]
                             ).then_inc(ada_ld[k], 16)

            for p in range(8):
                ada_piece(p)
            for B in range(2, NB):
                wait_unit(sp, ("xt", B - 2, 1))
                sp.dma_start(xs[B % 2], A["x"][0, P * B:P * B + P, :]).then_inc(x_ld[B % 2], 16)
            sp.dma_start(posi[:, 0:24], A["positions"]).then_inc(pos_ld, 16)
            for dst, name in ((c_ng, "norm_g"), (c_cb, "conv_b"), (c_lg, "conv_ln_g"), (c_lb, "conv_ln_b")):
                sp.dma_start(dst, A[name]).then_inc(const_ld, 16)
            sp.dma_start(c_gb, A["b_in_2_cols"][:, 10:26]).then_inc(const_ld, 16)
            sp.dma_start(c_ps, A["pool_scale_2"]).then_inc(const_ld, 16)
            sp.dma_start(c_pb, A["b_in_2_cols"][:, 0:4]).then_inc(const_ld, 16)
            sp.dma_start(c_ns, A["attn_sinks_2"].partition_broadcast(P).rearrange("p a h -> p (a h)")
                         ).then_inc(const_ld, 16)
            for p in range(8, 32):
                ada_piece(p)

            def mod_store(n):
                sp.wait_ge(ada_row, n + 1)
                sp.dma_start(mod_d[:, HALF * n:HALF * n + HALF], mrow[n % 3]).then_inc(mod_st[n % 3], 16)

            for n in range(4):
                mod_store(n)
            for n, v in enumerate((32, 16, 16)):
                sp.wait_ge(mod_st[n], v)
            sp.dma_start(c_sh, cols_of(mod_d[0, 0:D]), allow_slow_non_contiguous=True).then_inc(ada_col, 16)
            sp.dma_start(c_gs, cols_of(mod_d[0, D:2 * D]), allow_slow_non_contiguous=True).then_inc(ada_col, 16)
            for _ in range(8):
                next_piece()
            for p in range(32, 48):
                ada_piece(p)
            for n in (4, 5):
                mod_store(n)

            def conv_load(m):
                t, h = m // 2, m % 2
                if m >= 2:
                    sp.wait_ge(tap, TAPS * (m - 1))
                for hh in range(h + 1):
                    wait_stored(sp, ("ua", t, hh))
                if h == 0:
                    sp.dma_start(cu[0][:, 30:542], u_d[P * t:P * t + P, 0:HALF]).then_inc(u_ld[0], 16)
                else:
                    sp.dma_start(cu[1], u_d[P * t:P * t + P, HALF - 30:S]).then_inc(u_ld[1], 16)
                sp.dma_start(cw[m % 2], A["conv_w"][P * t:P * t + P, :]).then_inc(u_ld[m % 2], 16)

            def conv_store(m):
                t, h = m // 2, m % 2
                sp.wait_ge(tap, TAPS * (m + 1))
                sp.dma_start(feature_tile(c_d, t, h), ca).then_inc(c_st, 16)

            def conv_io(u):
                if u in taps_after:
                    a, b = taps_after[u]
                    for m in range(a // TAPS, b // TAPS):
                        conv_store(m)
                        if m + 2 < 16:
                            conv_load(m + 2)

            def store_heads(g, s):
                B, quad = s // 8, (s % 8) // 4
                a = 64 * g + s
                sp.wait_ge(o_out, a + 1)
                k = (a // 4) % 2
                cols = slice(256 * quad, 256 * quad + 256)
                if g == 0:
                    dst = [(slice(0, P), o_d[0][P * B:P * B + P, cols])]
                elif g == 1:
                    dst = [(slice(0, P), o_d[1].rearrange("(b i r) c -> b r i c", b=2, r=4)[B % 2, B // 2][:, cols])]
                else:
                    dst = [(slice(0, P), o_d[2].rearrange("(m b) c -> b m c", b=NB)[B][:, cols])]
                for rows, d in dst:
                    sp.dma_start(d, obuf[k][rows, :]).then_inc(ob_st[k], 16)

            def store_stats(g):
                sp.wait_ge(probs, 64 * g + 64)
                if g == 0:
                    dst = [(slice(0, P), stat[:, :, :], st_d[0].rearrange("(b i) c -> i b c", i=P))]
                elif g == 1:
                    dst = [(slice(0, P), stat[:, b:8:2, :],
                            st_d[1].rearrange("(b i r) c -> b i r c", b=2, r=4)[b]) for b in range(2)]
                else:
                    dst = [(slice(0, P), stat[:, :, :], st_d[2].rearrange("(m b) c -> m b c", b=NB))]
                for _, src, d in dst:
                    sp.dma_start(d, src).then_inc(stat_st, 16)

            DST = {"ua": u_d, "gc": gate_d["gc"], "ga": gate_d["ga"], "za": gate_d["za"], "zc": gate_d["zc"],
                   "g2p": gate_d["g2p"], "g2a": gate_d["g2a"]}

            def attention_io(g):
                per = att_share(len(ATT_STAGES[g]))
                us = att_units(g)
                for s in range(64):
                    for i in units_done(len(ATT_STAGES[g]), s):
                        u = us[i]
                        prefetch(u)
                        if i >= 1 and us[i - 1][0] in DST:
                            w = us[i - 1]
                            store_item(w, feature_tile(DST[w[0]], w[1], w[2]))
                        if i >= 1 and us[i - 1] == ("ua", 1, 1):
                            conv_load(0)
                            conv_load(1)
                    conv_io(("step", g, s))
                    if g < 3 and s >= 6 and (s - 6) % 4 == 1:
                        store_heads(g, s - 4)
                w = us[-1]
                store_item(w, feature_tile(DST[w[0]], w[1], w[2]))
                if g < 3:
                    store_heads(g, 63)
                    store_stats(g)

            def qkv_io(g):
                for u in STAGE_QKV[g]:
                    prefetch(u)
                    conv_io(u)

            for g in range(NG):
                qkv_io(g)
                attention_io(g)

            def conv_block(B):
                if B > 0:
                    wait_unit(sp, ("lt", B - 1, 1))
                sp.dma_start(cb.rearrange("p (k s) -> p k s", k=KT),
                             c_d.rearrange("(k p) s -> p k s", p=P)[:, :, P * B:P * B + P]).then_inc(cb_ld, 16)

            def attention_block(B):
                if B > 0:
                    wait_evac(sp, ("at", B - 1, 0))
                rows = slice(P * B, P * B + P)
                sp.dma_start(og_all, o_d[:, rows, :].rearrange("g p c -> p g c")).then_inc(o_ld, 16)
                sp.dma_start(sg, st_d[:, rows, :].rearrange("g p c -> p g c")).then_inc(o_ld, 16)
                sp.dma_start(zab.rearrange("p (k s) -> p k s", k=4),
                             gate_d["za"].rearrange("(k p) s -> p k s", p=P)[:, :, P * B:P * B + P]
                             ).then_inc(za_ld, 16)

            sp.wait_ge(c_st, 16 * 16)
            for n in range(2):
                sp.wait_ge(ob_st[n], OB_TOTAL[n])
            sp.wait_ge(stat_st, 16 * 4)
            for t in range(4):
                for h in range(2):
                    wait_stored(sp, ("za", t, h))
            sp.wait_ge(pv, 64 * NG)
            conv_block(0)
            attention_block(0)
            late = None
            for u in STAGE_Z:
                prefetch(u)
                if u[0] == "zc":
                    if late:
                        store_item(late, feature_tile(DST["zc"], late[1], late[2]))
                    late = u
                if u[0] == "lt" and u[2] == 1 and u[1] + 1 < NB:
                    conv_block(u[1] + 1)
                if u[0] == "at" and u[1] + 1 < NB:
                    attention_block(u[1] + 1)
            store_item(late, feature_tile(DST["zc"], late[1], late[2]))
            for t in range(8):
                if t == 0:
                    for tile in range(8):
                        for h in range(2):
                            wait_stored(sp, ("zc", tile, h))
                    wait_evac(sp, ("at", 7, 0))
                    wait_evac(sp, ("lt", 7, 1))
                if t >= 2:
                    sp.wait_ge(uz_w, t - 1)
                sp.dma_start(zt[t % 2], gate_d["zc"][P * t:P * t + P, :]).then_inc(z_ld[t % 2], 16)

            def gate_load(i, first, u, name):
                if i % 32 >= 4:
                    wait_evac(sp, GATED[i - 4])
                else:
                    sp.wait_ge(lo_done, SPLIT_LO[first])
                sp.dma_start(gt[i % 4], feature_tile(gate_d[name], u[1], u[2])).then_inc(g_ld[i % 4], 16)

            i = 0
            for u in units[U[("yc", 0, 0)]:U[("ya", 7, 1)] + 1]:
                prefetch(u)
                gate_load(i, ("uz", 7), u, "gc" if u[0] == "yc" else "ga")
                i += 1

            def norm_loads(r, names, first_gate):
                for n, src in enumerate(names):
                    sp.dma_start(bc[r][n], src).then_inc(bc_ld, 16)

            wait_unit(sp, ("ya", 7, 1))
            wait_evac(sp, ("ya", 7, 1))
            for n in range(3):
                sp.wait_ge(mod_st[n], 32)
            norm_loads(0, [mod_d[:, 2 * D:3 * D].partition_broadcast(P).rearrange("p a n -> p (a n)"),
                           A["final_g"].partition_broadcast(P), A["g_mix_pre_2"][0].partition_broadcast(P)], None)
            n = 0
            for h in range(2):
                for B in range(NB):
                    prefetch(("wo", B, h))
                    if n >= 2:
                        sp.wait_ge(n_x[0], n - 1)
                    sp.dma_start(xt2[n % 2], A["x"][0, P * B:P * B + P, HALF * h:HALF * h + HALF]
                                 ).then_inc(n_ld[0][n % 2], 16)
                    n += 1
                    if h and B >= 2:
                        sp.wait_ge(n_y[0], B - 1)
                        sp.dma_start(x1_d[P * (B - 2):P * (B - 1), :], tokT[:, B - 2, :]).then_inc(n_st[0], 16)
            for B in (6, 7):
                sp.wait_ge(n_y[0], B + 1)
                sp.dma_start(x1_d[P * B:P * B + P, :], tokT[:, B, :]).then_inc(n_st[0], 16)

            b2 = A["b_in_2"]
            for u in unit_range(("pl", 0, 0), ("pl", 3, 1)):
                prefetch(u)
            sp.wait_ge(n_st[0], 16 * 8)
            sp.wait_ge(n_xn[0], 8)
            sp.dma_start(bq_bc, b2[:, 512:1024].partition_broadcast(P).rearrange("p a n -> p (a n)")
                         ).then_inc(p_in, 16)
            sp.dma_start(bkv_bc, b2[:, 1024:1280].partition_broadcast(P).rearrange("p a n -> p (a n)")
                         ).then_inc(p_in, 16)
            sp.dma_start(wpool, A["w_pool_2"][0].rearrange("g c d -> c g d")).then_inc(p_in, 16)
            for u in unit_range(("q", 3, 0), ("kt", 3, 7)):
                prefetch(u)
            for t in range(4):
                for h in range(2):
                    wait_evac(sp, ("pm", t, h))
            sp.dma_start(yp_d.rearrange("(k p) s -> p k s", p=P), attzT).then_inc(yp_st, 16)
            attention_io(3)
            sp.wait_ge(y2_done, 8)
            sp.wait_ge(yp_st, 16)
            sp.dma_start(featT[:, 0:4, :], yp_d.rearrange("(k p) s -> p k s", p=P)).then_inc(yp_ld, 16)
            for n in ("g2p", "g2a"):
                for t in range(8):
                    for h in range(2):
                        wait_stored(sp, (n, t, h))
            for i, u in enumerate(unit_range(("yp", 0, 0), ("yb", 7, 1))):
                prefetch(u)
                gate_load(i + 32, ("y2", 3), u, "g2p" if u[0] == "yp" else "g2a")

            wait_evac(sp, ("yb", 7, 1))
            norm_loads(1, [A["g_mix_post_2"][0].partition_broadcast(P), A["g_mlp_pre_2"][0].partition_broadcast(P)],
                       None)
            sp.wait_ge(n_st[0], 16 * 8)
            for h in range(2):
                for B in range(NB):
                    prefetch(("w2", B, h))
                    if h:
                        if B >= 2:
                            sp.wait_ge(n_y[1], B - 1)
                        sp.dma_start(res[B % 2], x1_d[P * B:P * B + P, :]).then_inc(n_ld[1][B % 2], 16)
                        if B >= 2:
                            sp.dma_start(x2_d[P * (B - 2):P * (B - 1), :], tokT[:, B - 2, :]).then_inc(n_st[1], 16)
            for B in (6, 7):
                sp.wait_ge(n_y[1], B + 1)
                sp.dma_start(x2_d[P * B:P * B + P, :], tokT[:, B, :]).then_inc(n_st[1], 16)

            def mlp_pieces(src, j, before):
                for p in range(4):
                    sp.wait_ge(w_ready, before + p)
                    dst = raw[:, p, :].rearrange("p (k n) -> p k n", k=2) if src is up_src else raw[:, p, :]
                    sp.dma_start(dst, src(j, p)).then_inc(raw_ld[p], 16)

            mlp_pieces(up_src, 0, NP0 - 3)
            with sp.Fori(1, NJ) as k:
                mlp_pieces(up_src, k, NP0 + 8 * k - 7)
                mlp_pieces(down_src, k - 1, NP0 + 8 * k - 3)
            mlp_pieces(down_src, NJ - 1, NP0 + 8 * NJ - 7)

            sp.wait_ge(n_xn[1], 8)
            sp.dma_start(bc[2][0], A["g_mlp_post_2"][0].partition_broadcast(P)).then_inc(bc_ld, 16)
            sp.wait_ge(n_st[1], 16 * 8)
            sp.wait_ge(rel, 4 * NJ)
            sp.wait_ge(lo_done, len(SPLIT_LO) + 4 * NJ)
            for B in range(NB):
                if B >= 2:
                    sp.wait_ge(n_y[2], B - 1)
                sp.dma_start(res[B % 2], x2_d[P * B:P * B + P, :]).then_inc(n_ld[2][B % 2], 16)
                if B >= 2:
                    sp.dma_start(out[P * (B - 2):P * (B - 1), :], tokT[:, B - 2, :]).then_inc(out_st, 16)
            for B in (6, 7):
                sp.wait_ge(n_y[2], B + 1)
                sp.dma_start(out[P * B:P * B + P, :], tokT[:, B, :]).then_inc(out_st, 16)
            sp.wait_ge(out_st, 16 * NB)

        @block.gpsimd
        def _(pool):
            steps = [0]

            def link(ins):
                steps[0] += 1
                ins.then_inc(pool_step, 1)
                pool.wait_ge(pool_step, steps[0])

            pool.memset(epsc[:, 0:1], EPS).then_inc(eps_ready, 1)
            pool.memset(epsc[:, 1:2], 4 * EPS).then_inc(eps_ready, 1)
            link(pool.memset(ident[:, :], 0.0))
            link(pool.affine_select(out=ident[:, :], in_=ident[:, :], compare_op=ALU.not_equal, fill=1.0, base=0,
                                    pattern=[[-1, P]], channel_multiplier=1))
            link(pool.memset(band[:, :], 0.0))
            link(pool.affine_select(out=band[:, :], in_=band[:, :], compare_op=ALU.is_ge, fill=NEG, base=P,
                                    pattern=[[-1, 2 * P]], channel_multiplier=1))
            link(pool.affine_select(out=band[:, :], in_=band[:, :], compare_op=ALU.is_ge, fill=NEG, base=0,
                                    pattern=[[1, 2 * P]], channel_multiplier=-1))
            pool.iota(parity, pattern=[[-1, P]], base=P, channel_multiplier=1).then_inc(consts, 1)
            for t in range(15):
                link(pool.memset(small[:, 64 + t:65 + t], 1.0 / (t + 1)))
            link(pool.memset(cu[0][:, 0:30], 0.0))
            assert steps[0] == POOL_CONSTS
            pool.iota(posi[:, 24:32], pattern=[[P, 8]], base=0, channel_multiplier=1).then_inc(consts, 1)

            def split_piece(n, src, dhi, dlo):
                pool.tensor_copy(dhi, src).then_inc(w_hi_done, 1)
                pool.wait_ge(w_hi_done, n + 1)
                pool.tensor_tensor(dlo, src, dhi.bitcast(F32), ALU.subtract).then_inc(w_ready, 1)

            for n, (c, s) in enumerate(PIECES):
                pool.wait_ge(raw_ld[n % RAW], raw_total[n])
                if c >= 2 and s == 0:
                    pool.wait_ge(acc_ready, U[chunk_last[c - 2]] + 1)
                split_piece(n, raw[:, n % RAW, :], w_hi[:, c % 2, s, :], w_lo[:, c % 2, s, :])
                if chunks[c] == ("kv", 3) and s == 7:
                    pool.wait_ge(att_max, 64 * NG)
                    pool.affine_select(out=band[:, :], in_=band[:, :], compare_op=ALU.is_gt, fill=NEG, base=0,
                                       pattern=[[1, 2 * P]], channel_multiplier=-1).then_inc(consts, 1)

            def mlp_split(region, n0, ld, free):
                pool.wait_ge(acc_ready, free)
                for p in range(4):
                    pool.wait_ge(raw_ld[p], RAW_BASE[p] + 16 * (ld + 1))
                    pool.sem_inc(piece_seen)
                    split_piece(n0 + p, raw[:, p, :], w_hi[:, 0, region + p, :], w_lo[:, 0, region + p, :])

            mlp_split(0, NP0, 0, U[chunk_last[len(chunks) - 2]] + 1)
            mlp_split(0, NP0 + 4, 1, M0 + 4)
            mlp_split(4, NP0 + 8, 2, M0 + 4)
            with pool.Fori(2, NJ) as k:
                mlp_split(0, NP0 + 8 * k - 4, 2 * k - 1, M0 + 20 * k - 32)
                mlp_split(4, NP0 + 8 * k, 2 * k, M0 + 20 * k - 16)
            mlp_split(4, NP0 + 8 * NJ - 4, 2 * NJ - 1, M0 + 20 * NJ - 16)

        def silu_pair(u):
            return u[0] in ("za", "zc")

        @block.scalar
        def _(act):
            steps = [0]

            def step(ins):
                steps[0] += 1
                ins.then_inc(act_step, 1)

            def split_hi(key, dst, src):
                nc.scalar.activation(dst, src, ACT.Copy).then_inc(hi_done, 1)

            def copy_unit(u, dst):
                wait_unit(act, u)
                nc.scalar.activation(dst, bank(u), ACT.Copy).then_inc(free_of(u), 1)

            def transposed(u, dst):
                wait_unit(act, u)
                nc.scalar.activation(dst, bank(u).rearrange("p (k s) -> p k s", k=4), ACT.Copy
                                     ).then_inc(free_of(u), 1)

            for B in range(NB):
                act.wait_ge(x_ld[B % 2], 16 * (B // 2 + 1))
                nc.scalar.activation(act_lo[:, 0, :], xs[B % 2], ACT.Square,
                                     accum_out=tiny[:, B:B + 1]).then_inc(x_sq, 1)
                act.wait_ge(x_sq, 2 * B + 1)
                act.wait_ge(eps_ready, 2)
                nc.scalar.activation(tiny[:, 8 + B:9 + B], tiny[:, B:B + 1], ACT.Sqrt, scale=1.0 / D,
                                     bias=epsc[:, 0:1]).then_inc(x_sq, 1)
                if B >= 1:
                    for h in range(2):
                        transposed(("xt", B - 1, h), featT[:, 4 * h:4 * h + 4, P * (B - 1):P * B])
            for h in range(2):
                transposed(("xt", 7, h), featT[:, 4 * h:4 * h + 4, 7 * P:8 * P])
            act.wait_ge(ang_ready, 2)
            nc.scalar.activation(sinT[:, :, :].rearrange("p a j -> p (a j)"), angs, ACT.Sin).then_inc(rope_tab, 1)
            nc.scalar.activation(cosT[:, :, :].rearrange("p a j -> p (a j)"), angc, ACT.Sin).then_inc(rope_tab, 1)

            def ada_rows(n):
                act.wait_ge(ada_used, 8 * (n + 1))
                if n >= 3:
                    act.wait_ge(mod_st[n % 3], 16)
                nc.scalar.activation(mrow[n % 3], ps_s[n % 2][0:1, :], ACT.Copy).then_inc(ada_row, 1)

            for n in range(4):
                ada_rows(n)
            for k in range(KT):
                act.wait_ge(h_aff, k + 1)
                split_hi(("h", k), act_hi[:, k, :], featT[:, k, :])
            for n in (4, 5):
                ada_rows(n)

            def qkv_unit(u):
                name, g, B = u
                if name in "qk" and g < NG:
                    wait_slot(act, u)
                    copy_unit(u, slot(u))
                elif name == "v":
                    if B == 0 and g >= 1:
                        act.wait_ge(pv, 64 * g)
                    copy_unit(u, V[:, B, :])
                elif name in ("qt", "kt"):
                    if g >= 1 and g < NG and name == "qt" and B == 0:
                        act.wait_ge(scores, 64 * g)
                    wait_unit(act, u)
                    if g == 3 and name == "kt":
                        nc.scalar.activation(kT2[:, P * B:P * B + P], bank(u)[:, 0:P], ACT.Copy
                                             ).then_inc(free_of(u), 1)
                    else:
                        transposed(u, (qT if name == "qt" else kT)[:, :, P * B:P * B + P])
                elif name == "kv":
                    wait_evac(act, u)
                    nc.scalar.activation(V2[:, B, :], slot(("k", 3, B))[:, P:2 * P], ACT.Copy
                                         ).then_inc(v2_out, 1)

            def f_unit(u):
                name, t, h = u
                if name == "ub":
                    key = ("ua", t, h)
                    wait_slot(act, key)
                    wait_unit(act, u)
                    nc.scalar.activation(slot(key), bank(u), ACT.Tanh, scale=0.5).then_inc(free_of(u), 1)
                elif name in ("gc", "ga"):
                    wait_slot(act, u)
                    wait_unit(act, u)
                    nc.scalar.activation(slot(u), bank(u), ACT.Tanh, scale=0.5).then_inc(free_of(u), 1)
                elif name in ("g2p", "g2a"):
                    wait_slot(act, u)
                    wait_unit(act, u)
                    i = t + (8 if name == "g2a" else 0)
                    nc.scalar.activation(slot(u), bank(u), ACT.Tanh, scale=0.5, bias=c_gb[:, i:i + 1]
                                         ).then_inc(free_of(u), 1)
                elif silu_pair(u):
                    wait_slot(act, u)
                    wait_unit(act, u)
                    nc.scalar.activation(slot(u), bank(u), ACT.Tanh, scale=0.5).then_inc(tanh_done, 1)

            def exps(g, s):
                a = 64 * g + s
                B, h = s // 8, s % 8
                n = att_cfg(g, B)[1]
                act.wait_ge(att_max, a + 1)
                nc.scalar.activation(prob[a % 2][:, 0:n], prob[a % 2][:, 0:n], ACT.Exp, scale=-1.0,
                                     bias=stat[:, B, h:h + 1], accum_out=stat[:, B, 8 + h:9 + h]
                                     ).then_inc(probs, 1)

            def probs_out(g, s):
                a = 64 * g + s
                n = att_cfg(g, s // 8)[1]
                act.wait_ge(probs_t, a + 1)
                if a >= 2:
                    act.wait_ge(pv, a - 1)
                nc.scalar.activation(probT[a % 2][:, 0:n], ps_t[:, 0:n], ACT.Copy
                                     ).then_inc(pt_out, 1)

            def attention(g):
                us, C = att_units(g), len(ATT_STAGES[g])
                for s in range(65):
                    if s < 64:
                        for i in units_done(C, s):
                            f_unit(us[i])
                        exps(g, s)
                    if s >= 1:
                        probs_out(g, s - 1)

            for g in range(NG):
                for u in STAGE_QKV[g]:
                    qkv_unit(u)
                attention(g)

            def ln_root(B):
                act.wait_ge(ln_var, B + 1)
                nc.scalar.activation(tiny[:, 30:31], tiny[:, 29:30], ACT.Sqrt, bias=epsc[:, 1:2]
                                     ).then_inc(ln_sd, 1)
                act.wait_ge(ln_rs, B + 1)
                for h in range(2):
                    u = ("ct", B, h)
                    nc.scalar.activation(un[:, HALF * h:HALF * h + HALF], bank(u), ACT.Identity,
                                         scale=tiny[:, 31:32], bias=tiny[:, 32:33]).then_inc(free_of(u), 1)

            def weights_exp(B):
                act.wait_ge(cmb_m, B + 1)
                nc.scalar.activation(flat[:, 8:32], flat[:, 40:64], ACT.Exp).then_inc(cmb_e, 1)

            for u in STAGE_Z:
                name, B, h = u
                if name == "ct" and h == 1:
                    ln_root(B)
                    weights_exp(B)
                elif name == "zc":
                    f_unit(u)
                elif name == "lt":
                    transposed(u, featT[:, 4 * h:4 * h + 4, P * B:P * B + P])

            for k in range(KT + 1):
                if k < KT:
                    if k == 0:
                        for n in range(2):
                            act.wait_ge(z_ld[n], 16)
                    if k >= 2:
                        act.wait_ge(uz_w, k - 1)
                    nc.scalar.activation(tt[k % 2], featT[:, k, :], ACT.Tanh, scale=c_lgh[:, k:k + 1],
                                         bias=c_lbh[:, k:k + 1]).then_inc(uz_t, 1)
                if k >= 1:
                    act.wait_ge(uz_w, k)
                    if k == 1:
                        wait_unit(act, ("at", 7, 0))
                    split_hi(("uz", k - 1), act_hi[:, k - 1, :], featT[:, k - 1, :])

            wait_unit(act, ("yc", 7, 1))
            for k in range(4):
                split_hi(("az", k), act_hi[:, k, :], attzT[:, k, :])
            wait_unit(act, ("ya", 7, 1))
            for k in range(KT):
                act.wait_ge(mrg, 2 * k + 2)
                split_hi(("mg", k), act_hi[:, k, :], featT[:, k, :])

            def mean_square_root(r, B, at, signal):
                step(nc.scalar.activation(junk, tokT[:, B, :], ACT.Square, accum_out=flat[:, at + B:at + B + 1]))
                act.wait_ge(act_step, steps[0])
                nc.scalar.activation(flat[:, at + 8 + B:at + 9 + B], flat[:, at + B:at + B + 1], ACT.Sqrt,
                                     scale=1.0 / D, bias=epsc[:, 0:1]).then_inc(signal, 1)

            def norm_second(r, B):
                act.wait_ge(n_y[r], B + 1)
                mean_square_root(r, B, 16, n_s2[r])

            def normalise(r, name):
                for B in range(NB + 1):
                    if B < NB:
                        if r == 0:
                            act.wait_ge(n_x[0], NB + B + 1)
                        else:
                            wait_evac(act, ("w2", B, 1))
                        mean_square_root(r, B, 0, n_s1[r])
                    if B >= 1:
                        norm_second(r, B - 1)
                for B in range(NB):
                    for h in range(2):
                        wait_unit(act, (name, B, h))
                        split_hi((name, 2 * B + h), act_hi[:, 4 * h:4 * h + 4, P * B:P * B + P],
                                 bank((name, B, h)).rearrange("p (k s) -> p k s", k=4))

            normalise(0, "ht")

            for u in unit_range(("pl", 0, 0), ("pl", 3, 1)):
                wait_unit(act, u)
                nc.scalar.activation(attzT[:, u[1], HALF * u[2]:HALF * u[2] + HALF], bank(u), ACT.Identity,
                                     bias=c_pb[:, u[1]:u[1] + 1]).then_inc(free_of(u), 1)
            for u in unit_range(("q", 3, 0), ("kt", 3, 7)):
                qkv_unit(u)
            for u in unit_range(("pm", 0, 0), ("pm", 3, 1)):
                wait_unit(act, u)
                nc.scalar.activation(attzT[:, u[1], HALF * u[2]:HALF * u[2] + HALF], bank(u), ACT.Copy,
                                     scale=c_ps[:, u[1]:u[1] + 1]).then_inc(free_of(u), 1)
            us, C = att_units(3), len(ATT_STAGES[3])
            for s in range(67):
                if s < 64:
                    for i in units_done(C, s):
                        f_unit(us[i])
                    exps(3, s)
                if 1 <= s < 65:
                    probs_out(3, s - 1)
                if s > 2 and (s - 2) % 8 == 0:
                    B = (s - 2) // 8 - 1
                    act.wait_ge(y2_den, B + 1)
                    nc.scalar.activation(tiny[:, 8:16], tiny[:, 0:8], ACT.Exp).then_inc(y2_exp, 1)
            for B in range(NB):
                wait_unit(act, ("a2", B, 0))
                split_hi(("a2", B), act_hi[:, 0:4, P * B:P * B + P],
                         bank(("a2", B, 0)).rearrange("p (k s) -> p k s", k=4))
            act.wait_ge(yp_ld, 16)
            for k in range(4):
                split_hi(("y2", k), act_hi[:, 4 + k, :], featT[:, k, :])
            wait_unit(act, ("yb", 7, 1))
            for k in range(KT):
                act.wait_ge(mrg, 16 + 2 * k + 2)
                split_hi(("m2", k), act_hi[:, k, :], featT[:, k, :])
            normalise(1, "mt")

            def mlp_relu(k, i, n0, before):
                act.wait_ge(acc_ready, n0 + i + 1)
                if before is not None:
                    act.wait_ge(acc_free[i], before)
                nc.scalar.activation(relu[i], acc[i], ACT.Relu).then_inc(rel, 1)

            def mlp_hi(k, i, par, freed, down_done):
                act.wait_ge(acc_free[i], freed)
                if down_done is not None and i == 0:
                    act.wait_ge(acc_ready, down_done)
                nc.scalar.activation(hid[0][:, par, i // 2, HALF * (i % 2):HALF * (i % 2) + HALF], sq[i],
                                     ACT.Copy).then_inc(hi_done, 1)

            def mlp_up(k, par, n0, before, freed, down_done):
                for i in range(5):
                    if i < 4:
                        mlp_relu(k, i, n0, before)
                    if i >= 1:
                        mlp_hi(k, i - 1, par, freed, down_done)

            mlp_up(0, 0, M0, None, M4 + 1, None)
            mlp_up(1, 1, M0 + 4, M4 + 1, M4 + 2, None)
            with act.Fori(2, NJ, 2) as k:
                for par in range(2):
                    kk = k + par
                    mlp_up(kk, par, M0 + 20 * kk - 16, M4 + 5 * kk - 8, M4 + 5 * kk - 3, M0 + 20 * kk - 16)
            for B in range(NB):
                n = M0 + 20 * NJ - 16 + 2 * B + 1
                act.wait_ge(acc_free[n % ACC], n // ACC + 1)
                mean_square_root(2, B, 0, n_s1[2])

        @block.vector
        def _(dve):
            steps = [0]

            def step(ins):
                steps[0] += 1
                ins.then_inc(dve_step, 1)

            def settle():
                dve.wait_ge(dve_step, steps[0])

            def link(ins):
                step(ins)
                settle()

            def split_lo(key, dst, src, hi, signal=None):
                dve.wait_ge(hi_done, SPLIT[key])
                nc.vector.tensor_tensor(dst, src, hi.bitcast(F32), ALU.subtract).then_inc(lo_done, 1)

            for B in range(NB):
                dve.wait_ge(x_sq, 2 * B + 2)
                link(nc.vector.reciprocal(tiny[:, 8 + B:9 + B], tiny[:, 8 + B:9 + B]))
                nc.vector.tensor_scalar(xs[B % 2], xs[B % 2], tiny[:, 8 + B:9 + B], None, ALU.mult
                                        ).then_inc(x_norm, 1)

            freq = np.float32(THETA) ** (-(np.arange(8, dtype=np.float32) * np.float32(2.0 / 16)))
            C1 = 6.28125
            C2 = float(np.float32(np.round((2 * np.pi - C1) * 2.0 ** 20) / 2.0 ** 20))
            C3 = float(np.float32(2 * np.pi - C1 - C2))
            MAGIC = 1.5 * 2.0 ** 23
            dve.wait_ge(pos_ld, 16)
            dve.wait_ge(consts, 2)
            dve.wait_ge(pool_step, POOL_CONSTS)
            link(nc.vector.tensor_single_scalar(parity, parity, 1, ALU.bitwise_and))
            link(nc.vector.tensor_copy(resid[:, :], parity))
            link(nc.vector.scalar_tensor_tensor(resid[:, :], resid[:, :], NEG, band[:, P:2 * P], ALU.mult, ALU.add))
            wait_unit(dve, ("xt", 7, 1))
            link(nc.vector.tensor_copy(posf, posi))
            for j in range(8):
                step(nc.vector.tensor_scalar(angr[:, :, j], posf, float(freq[j]), None, ALU.mult))
            settle()
            for shift, dst in ((0.0, angs), (0.25, angc)):
                link(nc.vector.tensor_scalar(turns, ang, 1.0 / (2 * np.pi), shift, ALU.mult, ALU.add))
                link(nc.vector.tensor_scalar(turns, turns, MAGIC, None, ALU.add))
                link(nc.vector.tensor_scalar(turns, turns, -MAGIC, None, ALU.add))
                link(nc.vector.scalar_tensor_tensor(dst, turns, -C1, ang, ALU.mult, ALU.add))
                link(nc.vector.scalar_tensor_tensor(dst, turns, -C2, dst, ALU.mult, ALU.add))
                link(nc.vector.scalar_tensor_tensor(dst, turns, -C3, dst, ALU.mult, ALU.add))
                if shift:
                    link(nc.vector.tensor_scalar(dst, dst, float(np.float32(np.pi / 2)), None, ALU.add))
                nc.vector.tensor_scalar(dst, dst, 3.1415925, -3.1415925, ALU.min, ALU.max).then_inc(ang_ready, 1)

            dve.wait_ge(const_ld, 16 * 8)
            step(nc.vector.tensor_scalar(c_cb, c_cb, 2.0, None, ALU.mult))
            step(nc.vector.tensor_scalar(c_lgh, c_lg, 0.5, None, ALU.mult))
            step(nc.vector.tensor_scalar(c_lbh, c_lb, 0.5, None, ALU.mult))
            step(nc.vector.tensor_scalar(c_gb, c_gb, 0.5, None, ALU.mult))
            step(nc.vector.tensor_scalar(c_ns, c_ns, -1.0, None, ALU.mult))
            dve.wait_ge(ada_col, 32)
            link(nc.vector.scalar_tensor_tensor(c_gs, c_gs, 1.0, c_ng, ALU.add, ALU.mult))

            wait_evac(dve, ("xt", 7, 1))
            for k in range(KT + 1):
                if k < KT:
                    nc.vector.tensor_scalar(featT[:, k, :], featT[:, k, :], c_gs[:, k:k + 1], c_sh[:, k:k + 1],
                                            ALU.mult, ALU.add).then_inc(h_aff, 1)
                if k >= 1:
                    split_lo(("h", k - 1), act_lo[:, k - 1, :], featT[:, k - 1, :], act_hi[:, k - 1, :])

            def rotate(u, heads):
                name, g, B = u
                t = slot(u)[:, 0:heads * HD].rearrange("p (h c) -> p h c", c=HD)[:, :, 0:16]
                t4 = t.rearrange("p h (i j) -> p h i j", i=2)
                tx = rx[:, 0:heads * 16].rearrange("p (h i j) -> p h i j", i=2, j=8)
                ty = ry[:, 0:heads * 16].rearrange("p (h i j) -> p h i j", i=2, j=8)
                n = 8 * g + B
                c, s = (tab[:, n:n + 1, :].unsqueeze(1).to_broadcast([P, heads, 2, 8]) for tab in (cosT, sinT))
                step(nc.vector.tensor_tensor(tx, t4, c, ALU.mult))
                link(nc.vector.tensor_tensor(ty, t4, s, ALU.mult))
                step(nc.vector.tensor_tensor(t[:, :, 0:8], tx[:, :, 0, :], ty[:, :, 1, :], ALU.subtract))
                nc.vector.tensor_tensor(t[:, :, 8:16], tx[:, :, 1, :], ty[:, :, 0, :], ALU.add
                                        ).then_inc(roped, 1)
                dve.wait_ge(roped, ROPE[u])

            def conv_taps(u):
                for t in range(*taps_after.get(u, (0, 0))):
                    m, j = t // TAPS, t % TAPS
                    u_in, w = cu[m % 2], cw[m % 2]
                    if j == 0:
                        dve.wait_ge(u_ld[m % 2], 32 * (m // 2 + 1))
                        if m:
                            dve.wait_ge(c_st, 16 * m)
                        nc.vector.tensor_scalar(ca, u_in[:, 0:HALF], w[:, 0:1], c_cb[:, m // 2:m // 2 + 1],
                                                ALU.mult, ALU.add).then_inc(tap, 1)
                    else:
                        dve.wait_ge(tap, t)
                        nc.vector.scalar_tensor_tensor(ca, u_in[:, j:j + HALF], w[:, j:j + 1], ca,
                                                       ALU.mult, ALU.add).then_inc(tap, 1)

            def f_unit(u):
                name, t, h = u
                if name == "ua":
                    wait_evac(dve, ("ub", t, h))
                    wait_unit(dve, u)
                    nc.vector.scalar_tensor_tensor(slot(u), slot(u), 1.0, bank(u), ALU.add, ALU.mult
                                                   ).then_inc(free_of(u), 1)
                elif silu_pair(u):
                    dve.wait_ge(tanh_done, TANH[u])
                    nc.vector.scalar_tensor_tensor(slot(u), slot(u), 1.0, bank(u), ALU.add, ALU.mult
                                                   ).then_inc(free_of(u), 1)

            def score_max(g, s):
                a = 64 * g + s
                B, h = s // 8, s % 8
                _, n, mask = att_cfg(g, B)
                dve.wait_ge(scores, a + 1)
                if a >= 2:
                    dve.wait_ge(probs_t, a - 1)
                nc.vector.tensor_tensor_reduce(prob[a % 2][:, 0:n], ps_s[a % 2][:, 0:n], mask, -0.125,
                                               c_ns[:, h:h + 1] if g == 3 else 1e30, ALU.add, ALU.min,
                                               stat[:, B, h:h + 1]).then_inc(att_max, 1)

            def out_head(g, s):
                a = 64 * g + s
                B, h = s // 8, s % 8
                dve.wait_ge(pv, a + 1)
                src = ps_o[:, 0:HD]
                if g == 3:
                    nc.vector.tensor_copy(yv[:, B, 64 * h:64 * h + 64], src).then_inc(o_out, 1)
                    return
                quad = a // 4
                if a % 4 == 0 and quad >= 2:
                    dve.wait_ge(ob_st[quad % 2], ob_count(quad))
                nc.vector.tensor_copy(obuf[quad % 2][:, 64 * (h % 4):64 * (h % 4) + 64], src).then_inc(o_out, 1)

            def attention(g):
                us, C = att_units(g), len(ATT_STAGES[g])
                if g >= 1:
                    dve.wait_ge(stat_st, 16 * (1, 3)[g - 1])
                for s in range(66):
                    if s < 64:
                        score_max(g, s)
                    if s >= 2:
                        out_head(g, s - 2)
                    if s < 64:
                        for i in units_done(C, s):
                            f_unit(us[i])
                        if g < NG:
                            conv_taps(("step", g, s))

            for g in range(NG):
                if g:
                    dve.wait_ge(probs_t, 64 * g)
                else:
                    dve.wait_ge(rope_tab, 2)
                for u in STAGE_QKV[g]:
                    if u[0] in "qk":
                        wait_evac(dve, u)
                        rotate(u, HPG)
                    conv_taps(u)
                attention(g)

            bn, mv = tiny[:, 16:28], tiny[:, 28:30]

            def ln_stats(B, h):
                wait_unit(dve, ("ct", B, h))
                step(nc.vector.bn_stats(bn[:, 6 * h:6 * h + 6], bank(("ct", B, h))))
                if h == 1:
                    settle()
                    nc.vector.bn_aggr(mv, bn).then_inc(ln_var, 1)

            def ln_scale(B):
                dve.wait_ge(ln_sd, B + 1)
                link(nc.vector.reciprocal(tiny[:, 31:32], tiny[:, 30:31]))
                nc.vector.scalar_tensor_tensor(tiny[:, 32:33], mv[:, 0:1], -1.0, tiny[:, 31:32], ALU.mult, ALU.mult
                                               ).then_inc(ln_rs, 1)

            def weights_max(B):
                dve.wait_ge(o_ld, 32 * (B + 1))
                link(nc.vector.tensor_tensor(flat[:, 0:8], sg[:, 0, 0:8], sg[:, 1, 0:8], ALU.min))
                link(nc.vector.tensor_tensor(flat[:, 0:8], flat[:, 0:8], sg[:, 2, 0:8], ALU.min))
                nc.vector.tensor_tensor(flat[:, 40:64].rearrange("p (g h) -> p g h", g=NG),
                                        flat[:, 0:8].unsqueeze(1).to_broadcast([P, NG, 8]), sg[:, :, 0:8],
                                        ALU.subtract).then_inc(cmb_m, 1)

            def combine(B):
                dve.wait_ge(cmb_e, B + 1)
                e = flat[:, 8:32].rearrange("p (g h) -> p g h", g=NG)
                d = flat[:, 64:88].rearrange("p (g h) -> p g h", g=NG)
                link(nc.vector.tensor_tensor(d, e, sg[:, :, 8:16], ALU.mult))
                link(nc.vector.tensor_tensor(flat[:, 96:104], d[:, 0, :], d[:, 1, :], ALU.add))
                link(nc.vector.tensor_tensor(flat[:, 96:104], flat[:, 96:104], d[:, 2, :], ALU.add))
                link(nc.vector.reciprocal(flat[:, 104:112], flat[:, 96:104]))
                link(nc.vector.tensor_tensor(e, e, flat[:, 104:112].unsqueeze(1).to_broadcast([P, NG, 8]), ALU.mult))
                for g in range(NG):
                    o = og[g].rearrange("p (h c) -> p h c", c=HD)
                    step(nc.vector.tensor_tensor(o, o, e[:, g, :].unsqueeze(2).to_broadcast([P, 8, HD]), ALU.mult))
                settle()
                link(nc.vector.tensor_tensor(og[0], og[0], og[1], ALU.add))
                nc.vector.tensor_tensor(og[0], og[0], og[2], ALU.add).then_inc(att_done, 1)

            for u in STAGE_Z:
                name, B, h = u
                if name == "ct":
                    ln_stats(B, h)
                    if h == 1:
                        ln_scale(B)
                        weights_max(B)
                        combine(B)
                elif name == "zc":
                    f_unit(u)
                elif name == "at":
                    wait_unit(dve, u)
                    dve.wait_ge(za_ld, 16 * (B + 1))
                    nc.vector.scalar_tensor_tensor(
                        attzT[:, :, P * B:P * B + P], bank(u).rearrange("p (k s) -> p k s", k=4), 0.5,
                        zab.rearrange("p (k s) -> p k s", k=4), ALU.mult, ALU.mult).then_inc(free_of(u), 1)

            for k in range(KT + 1):
                if k < KT:
                    x = featT[:, k, :]
                    dve.wait_ge(uz_t, k + 1)
                    link(nc.vector.tensor_scalar(x, x, c_lg[:, k:k + 1], c_lb[:, k:k + 1], ALU.mult, ALU.add))
                    link(nc.vector.scalar_tensor_tensor(x, tt[k % 2], 1.0, x, ALU.add, ALU.mult))
                    dve.wait_ge(z_ld[k % 2], 16 * (k // 2 + 1))
                    nc.vector.scalar_tensor_tensor(x, x, 0.25, zt[k % 2], ALU.mult, ALU.mult).then_inc(uz_w, 1)
                if k >= 1:
                    split_lo(("uz", k - 1), act_lo[:, k - 1, :], featT[:, k - 1, :], act_hi[:, k - 1, :])

            def gated(i, u, add):
                name, t, h = u
                dst = featT[:, t, HALF * h:HALF * h + HALF]
                wait_unit(dve, u)
                dve.wait_ge(g_ld[i % 4], 16 * (i // 4 + 1))
                if not add:
                    nc.vector.scalar_tensor_tensor(dst, gt[i % 4], 1.0, bank(u), ALU.add, ALU.mult
                                                   ).then_inc(free_of(u), 1)
                    return
                nc.vector.scalar_tensor_tensor(gtmp[i % 2], gt[i % 4], 1.0, bank(u), ALU.add, ALU.mult
                                               ).then_inc(free_of(u), 1)
                wait_evac(dve, u)
                nc.vector.tensor_tensor(dst, dst, gtmp[i % 2], ALU.add).then_inc(mrg, 1)

            def branches(i0, first, second, key):
                i = i0
                for t in range(8):
                    for h in range(2):
                        gated(i, (first, t, h), False)
                        i += 1
                if key == "az":
                    for k in range(4):
                        split_lo(("az", k), act_lo[:, k, :], attzT[:, k, :], act_hi[:, k, :])
                for t in range(8):
                    for h in range(2):
                        gated(i, (second, t, h), True)
                        i += 1

            branches(0, "yc", "ya", "az")
            for k in range(KT):
                split_lo(("mg", k), act_lo[:, k, :], featT[:, k, :], act_hi[:, k, :])

            def evac_out(r, B, h, n):
                u = (("wo", "w2")[r], B, h)
                dst = tokT[:, B, HALF * h:HALF * h + HALF]
                wait_unit(dve, u)
                if r == 1:
                    nc.vector.tensor_scalar(dst, bank(u), 0.5, None, ALU.mult).then_inc(free_of(u), 1)
                    return
                nc.vector.scalar_tensor_tensor(dst, bank(u), 0.5, bc[0][0][:, HALF * h:HALF * h + HALF],
                                               ALU.mult, ALU.mult).then_inc(free_of(u), 1)
                wait_evac(dve, u)
                dve.wait_ge(n_ld[0][n % 2], 16 * (n // 2 + 1))
                nc.vector.tensor_tensor(dst, dst, xt2[n % 2], ALU.add).then_inc(n_x[0], 1)

            def norm_one(r, B):
                dve.wait_ge(n_s1[r], B + 1)
                link(nc.vector.reciprocal(flat[:, 8 + B:9 + B], flat[:, 8 + B:9 + B]))
                ins = nc.vector.scalar_tensor_tensor(tokT[:, B, :], tokT[:, B, :], flat[:, 8 + B:9 + B],
                                                     bc[r][1 if r == 0 else 0], ALU.mult, ALU.mult)
                if r:
                    link(ins)
                    dve.wait_ge(n_ld[r][B % 2], 16 * (B // 2 + 1))
                    ins = nc.vector.tensor_tensor(tokT[:, B, :], tokT[:, B, :], res[B % 2], ALU.add)
                ins.then_inc(n_y[r], 1)

            def norm_two(r, B):
                dve.wait_ge(n_s2[r], B + 1)
                link(nc.vector.reciprocal(flat[:, 24 + B:25 + B], flat[:, 24 + B:25 + B]))
                if B >= 2:
                    wait_unit(dve, (("ht", "mt")[r], B - 2, 1))
                nc.vector.scalar_tensor_tensor(xn[B % 2], tokT[:, B, :], flat[:, 24 + B:25 + B],
                                               bc[r][2 if r == 0 else 1], ALU.mult, ALU.mult).then_inc(n_xn[r], 1)

            def normalise(r, name):
                dve.wait_ge(bc_ld, (48, 80)[r])
                for B in range(NB):
                    evac_out(r, B, 0, B)
                for B in range(NB + 2):
                    if B < NB:
                        evac_out(r, B, 1, NB + B)
                    if 1 <= B <= NB:
                        norm_one(r, B - 1)
                    if 2 <= B < 4:
                        norm_two(r, B - 2)
                for B in range(NB):
                    for h in range(2):
                        u = (name, B, h)
                        dve.wait_ge(hi_done, SPLIT[(name, 2 * B + h)])
                        cols = slice(P * B, P * B + P)
                        nc.vector.tensor_tensor(act_lo[:, 4 * h:4 * h + 4, cols],
                                                bank(u).rearrange("p (k s) -> p k s", k=4),
                                                act_hi[:, 4 * h:4 * h + 4, cols].bitcast(F32), ALU.subtract
                                                ).then_inc(free_of(u), 1)
                    if B + 2 < NB:
                        norm_two(r, B + 2)

            normalise(0, "ht")

            def pooling(t):
                u, w = attzT[:, t, :], POOL_W[t]
                wait_evac(dve, ("pl", t, 1))
                src, buf = u, 0
                for lv in range(t + 1):
                    sh, dst = 1 << lv, pw[buf]
                    step(nc.vector.tensor_tensor(dst[:, sh:S], src[:, sh:S], src[:, 0:S - sh], ALU.add))
                    link(nc.vector.tensor_copy(dst[:, 0:sh], src[:, 0:sh]))
                    src, buf = dst, 1 - buf
                link(nc.vector.tensor_tensor(src[:, 0:w - 1], src[:, 0:w - 1], small[:, 64:64 + w - 1], ALU.mult))
                step(nc.vector.tensor_tensor(u[:, 0:w - 1], src[:, 0:w - 1], u[:, 0:w - 1], ALU.subtract))
                nc.vector.scalar_tensor_tensor(u[:, w - 1:S], src[:, w - 1:S], 1.0 / w, u[:, w - 1:S],
                                               ALU.mult, ALU.subtract).then_inc(p_diff, 1)
                dve.wait_ge(p_diff, t + 1)

            dve.wait_ge(p_in, 48)
            for u in unit_range(("q", 3, 0), ("kt", 3, 7)):
                name, _, B = u
                if name == "q":
                    wait_slot(dve, u)
                    wait_unit(dve, u)
                    nc.vector.tensor_tensor(slot(u).rearrange("p (h a e) -> p a h e", h=4, a=2),
                                            bank(u).rearrange("p (a h e) -> p a h e", h=4, a=2),
                                            bq_bc.rearrange("p (a h e) -> p a h e", h=4, a=2), ALU.add
                                            ).then_inc(free_of(u), 1)
                    wait_evac(dve, u)
                    rotate(u, 8)
                    if B % 2:
                        pooling(B // 2)
                elif name == "kv":
                    key = ("k", 3, B)
                    wait_slot(dve, key)
                    if B >= EVN:
                        dve.wait_ge(v2_out, B - EVN + 1)
                    wait_unit(dve, u)
                    nc.vector.tensor_tensor(slot(key)[:, 0:256], bank(u)[:, 0:256], bkv_bc, ALU.add
                                            ).then_inc(free_of(u), 1)
                    wait_evac(dve, u)
                    rotate(key, 2)
            dve.wait_ge(consts, 3)
            dve.wait_ge(yp_st, 16)
            for s in range(69):
                if s < 64:
                    score_max(3, s)
                if 2 <= s < 66:
                    out_head(3, s - 2)
                    if (s - 2) % 8 == 7:
                        B = (s - 2) // 8
                        nc.vector.tensor_tensor(tiny[:, 0:8], stat[:, B, 0:8], c_ns, ALU.subtract
                                                ).then_inc(y2_den, 1)
                if s >= 12 and (s - 12) % 8 == 0:
                    B = (s - 12) // 8
                    dve.wait_ge(y2_exp, B + 1)
                    link(nc.vector.tensor_tensor(tiny[:, 16:24], stat[:, B, 8:16], tiny[:, 8:16], ALU.add))
                    link(nc.vector.reciprocal(tiny[:, 16:24], tiny[:, 16:24]))
                    y = yv[:, B, :].rearrange("p (h c) -> p h c", c=HD)
                    dve.wait_ge(o_out, 64 * 3 + 8 * B + 8)
                    nc.vector.tensor_tensor(y, y, tiny[:, 16:24].unsqueeze(2).to_broadcast([P, 8, HD]), ALU.mult
                                            ).then_inc(y2_done, 1)
            for B in range(NB):
                u = ("a2", B, 0)
                dve.wait_ge(hi_done, SPLIT[("a2", B)])
                cols = slice(P * B, P * B + P)
                nc.vector.tensor_tensor(act_lo[:, 0:4, cols], bank(u).rearrange("p (k s) -> p k s", k=4),
                                        act_hi[:, 0:4, cols].bitcast(F32), ALU.subtract).then_inc(free_of(u), 1)
            for k in range(4):
                split_lo(("y2", k), act_lo[:, 4 + k, :], featT[:, k, :], act_hi[:, 4 + k, :])
            branches(32, "yp", "yb", None)
            for k in range(KT):
                split_lo(("m2", k), act_lo[:, k, :], featT[:, k, :], act_hi[:, k, :])
            normalise(1, "mt")

            NS = len(splits)

            def mlp_square(k, par):
                for i in range(5):
                    if i < 4:
                        dve.wait_ge(rel, 4 * k + i + 1)
                        nc.vector.tensor_tensor(sq[i], relu[i], acc[i], ALU.mult).then_inc(acc_free[i], 1)
                    if i >= 1:
                        dve.wait_ge(hi_done, 4 * k + (NS + i))
                        t, h = (i - 1) // 2, (i - 1) % 2
                        cols = slice(HALF * h, HALF * h + HALF)
                        nc.vector.tensor_tensor(hid[1][:, par, t, cols], sq[i - 1],
                                                hid[0][:, par, t, cols].bitcast(F32), ALU.subtract
                                                ).then_inc(lo_done, 1)

            def mlp_add(j, n0, first, before):
                dve.wait_ge(acc_free[3], before)
                for i in range(16):
                    dst = tokT[:, i // 2, HALF * (i % 2):HALF * (i % 2) + HALF]
                    dve.wait_ge(acc_ready, n0 + (i + 1))
                    if first:
                        ins = nc.vector.tensor_copy(dst, acc[i % ACC])
                    else:
                        ins = nc.vector.tensor_tensor(dst, dst, acc[i % ACC], ALU.add)
                    ins.then_inc(acc_free[i % ACC], 1)

            mlp_square(0, 0)
            mlp_square(1, 1)
            dve.wait_ge(n_st[1], 16 * NB)
            mlp_add(0, M0 + 8, True, M4 + 2)
            with dve.Fori(2, NJ, 2) as k:
                for par in range(2):
                    kk = k + par
                    mlp_square(kk, par)
                    mlp_add(kk - 1, M0 + 20 * kk - 12, False, M4 + 5 * kk - 3)
            mlp_add(NJ - 1, M0 + 20 * NJ - 16, False, M4 + 5 * NJ - 4)
            dve.wait_ge(bc_ld, 96)
            for B in range(NB):
                norm_one(2, B)

        @block.tensor
        def _(pe):
            PARTS = [(0, 0), (0, 1), (1, 0)]
            act_p, w_p = (act_hi, act_lo), (w_hi, w_lo)
            FIRST = {"q0": "h", "yc": "uz", "ya": "az", "wo": "mg", "pl": "ht", "yp": "y2", "w2": "m2"}

            def begin(u):
                if U[u] >= ACC:
                    pe.wait_ge(free_of(u), U[u] // ACC)

            def proj(u, m):
                name, t, h = u
                c, i = unit_chunk[u]
                k, (a, b) = m // 3, PARTS[m % 3]
                nk = 4 if name in ("ya", "yp", "yb") else 8
                if m == 0:
                    begin(u)
                if i == 0 and m % 3 == 0:
                    pe.wait_ge(w_ready, 8 * c + (8 // nk) * (k + 1))
                    key = FIRST.get("q0" if (name, t) == ("q", 0) else name)
                    if key and chunks[c][1] == 0:
                        if key == "ht":
                            wait_evac(pe, ("ht", 7, 1))
                        else:
                            pe.wait_ge(lo_done, SPLIT_LO[(key, k)])
                s = c % 2
                if name in ("q", "k", "v", "kv", "wo", "w2"):
                    g, B = (t, h) if name in ("q", "k", "v", "kv") else (0, t)
                    n = 256 if name == "kv" else HALF
                    blk = token_block(g, B)
                    out_, lhs, rhs = bank(u)[:, 0:n], blk(act_p[a][:, k, :]), w_p[b][:, s, k, 0:n]
                else:
                    if nk == 4:
                        sub, c0 = 2 * k + t // 4, P * (t % 4)
                    elif name in ("ua", "ub"):
                        sub, c0 = k, P * (t % 2) + (256 if name == "ub" else 0)
                    else:
                        sub, c0 = k, P * (t % 4)
                    kk = k + 4 if name == "yp" else k
                    out_, lhs = bank(u), w_p[b][:, s, sub, c0:c0 + P]
                    rhs = act_p[a][:, kk, HALF * h:HALF * h + HALF]
                ins = nc.tensor.matmul(out_, lhs, rhs, start=(m == 0), stop=(m == 3 * nk - 1))
                if m == 3 * nk - 1:
                    ins.then_inc(acc_ready, 1)

            def project(u):
                for m in range(12 if u[0] in ("ya", "yp", "yb") else 24):
                    proj(u, m)

            def turn(u, srcs):
                begin(u)
                for i, src in enumerate(srcs):
                    ins = nc.tensor.transpose(bank(u)[:, P * i:P * i + P], src, ident[:, :])
                ins.then_inc(acc_ready, 1)

            pe.wait_ge(pool_step, 2)
            for B in range(NB):
                pe.wait_ge(x_norm, B + 1)
                for h in range(2):
                    turn(("xt", B, h), [xs[B % 2][:, P * i:P * i + P] for i in range(4 * h, 4 * h + 4)])

            def ada_row_(n):
                out_ = ps_s[n % 2][0:1, :]
                if n >= 2:
                    pe.wait_ge(ada_row, n - 1)
                nc.tensor.matmul(out_, ident[0:6, n:n + 1], bada, start=True, stop=False)
                for k in range(KT):
                    pe.wait_ge(ada_ld[k], 16 * (n + 1))
                    nc.tensor.matmul(out_, small[:, k:k + 1], ada[:, k, :], start=False, stop=(k == KT - 1)
                                     ).then_inc(ada_used, 1)

            pe.wait_ge(c_ld, 32)
            for n in range(6):
                ada_row_(n)

            def qkv_unit(u):
                name, g, B = u
                if name in ("qt", "kt"):
                    key = (name[0], g, B)
                    pe.wait_ge(roped, ROPE[key])
                    buf = slot(key)
                    if (name, g) == ("kt", 3):
                        turn(u, [buf[:, 0:P]])
                    else:
                        turn(u, [buf[:, P * i:P * i + P] for i in range(4)])
                else:
                    project(u)

            def score(g, s):
                a = 64 * g + s
                B, h = s // 8, s % 8
                k0, n, _ = att_cfg(g, B)
                pair, half = (h // 2, h % 2) if g < 3 else (h % 4, h // 4)
                rows = slice(64 * half, 64 * half + 64)
                if a >= 2:
                    pe.wait_ge(att_max, a - 1)
                keys = kT[rows, pair, k0:k0 + n] if g < 3 else kT2[rows, k0:k0 + n]
                nc.tensor.matmul(ps_s[a % 2][:, 0:n], qT[rows, pair, P * B:P * B + P], keys, start=True, stop=True
                                 ).then_inc(scores, 1)

            def prob_t(g, s):
                a = 64 * g + s
                n = att_cfg(g, s // 8)[1]
                pe.wait_ge(probs, a + 1)
                if a >= 1:
                    pe.wait_ge(pt_out, a)
                for i in range(n // P):
                    ins = nc.tensor.transpose(ps_t[:, P * i:P * i + P],
                                              prob[a % 2][:, P * i:P * i + P], ident[:, :])
                ins.then_inc(probs_t, 1)

            def prob_v(g, s):
                a = 64 * g + s
                B, h = s // 8, s % 8
                k0, n, _ = att_cfg(g, B)
                pe.wait_ge(pt_out, a + 1)
                if a >= 1:
                    pe.wait_ge(o_out, a)
                for i in range(n // P):
                    v = (V[:, k0 // P + i, 64 * h:64 * h + 64] if g < 3
                         else V2[:, k0 // P + i, 64 * (h // 4):64 * (h // 4) + 64])
                    ins = nc.tensor.matmul(ps_o[:, 0:HD],
                                           probT[a % 2][:, P * i:P * i + P], v, start=(i == 0),
                                           stop=(i == n // P - 1))
                ins.then_inc(pv, 1)

            def attention(g):
                us, per = att_units(g), att_share(len(ATT_STAGES[g]))
                for s in range(66):
                    if s < 64:
                        for m in range(s * per, (s + 1) * per):
                            proj(us[m // 24], m % 24)
                        score(g, s)
                    if 1 <= s < 65:
                        prob_t(g, s - 1)
                    if s >= 2:
                        prob_v(g, s - 2)

            for g in range(NG):
                for u in STAGE_QKV[g]:
                    qkv_unit(u)
                wait_evac(pe, ("v", g, 7))
                attention(g)

            for u in STAGE_Z:
                name, B, h = u
                if name == "ct":
                    pe.wait_ge(cb_ld, 16 * (B + 1))
                    turn(u, [cb[:, P * i:P * i + P] for i in range(4 * h, 4 * h + 4)])
                elif name == "at":
                    pe.wait_ge(att_done, B + 1)
                    turn(u, [og[0][:, P * i:P * i + P] for i in range(4)])
                elif name == "lt":
                    wait_evac(pe, ("ct", B, h))
                    turn(u, [un[:, P * i:P * i + P] for i in range(4 * h, 4 * h + 4)])
                else:
                    project(u)
            for u in unit_range(("yc", 0, 0), ("wo", 7, 1)):
                project(u)

            def turn_norm(r, name):
                for B in range(NB):
                    pe.wait_ge(n_xn[r], B + 1)
                    for h in range(2):
                        turn((name, B, h), [xn[B % 2][:, P * i:P * i + P] for i in range(4 * h, 4 * h + 4)])

            turn_norm(0, "ht")

            for u in unit_range(("pl", 0, 0), ("kt", 3, 7)):
                qkv_unit(u)
            for u in unit_range(("pm", 0, 0), ("pm", 3, 1)):
                begin(u)
                pe.wait_ge(p_diff, u[1] + 1)
                nc.tensor.matmul(bank(u), wpool[:, u[1], :], attzT[:, u[1], HALF * u[2]:HALF * u[2] + HALF],
                                 start=True, stop=True).then_inc(acc_ready, 1)
            pe.wait_ge(v2_out, 8)
            wait_evac(pe, ("kt", 3, 7))
            attention(3)
            for B in range(NB):
                pe.wait_ge(y2_done, B + 1)
                turn(("a2", B, 0), [yv[:, B, P * i:P * i + P] for i in range(4)])
            for u in unit_range(("yp", 0, 0), ("w2", 7, 1)):
                project(u)
            turn_norm(1, "mt")

            def up(bank_free, weights):
                pe.wait_ge(w_ready, weights)
                for i in range(4):
                    t, h = i // 2, i % 2
                    pe.wait_ge(acc_free[i], bank_free)
                    for m in range(24):
                        k, (a, b) = m // 3, PARTS[m % 3]
                        ins = nc.tensor.matmul(acc[i], up_w[b][:, k, P * t:P * t + P],
                                               act_p[a][:, k, HALF * h:HALF * h + HALF],
                                               start=(m == 0), stop=(m == 23))
                    ins.then_inc(acc_ready, 1)

            def down(j, par, bank_free, weights):
                pe.wait_ge(w_ready, weights)
                pe.wait_ge(lo_done, len(SPLIT_LO) + 4 + 4 * j)
                for i in range(16):
                    B, h = i // 2, i % 2
                    pe.wait_ge(acc_free[i % ACC], bank_free + i // ACC)
                    for m in range(6):
                        k, (a, b) = m // 3, PARTS[m % 3]
                        ins = nc.tensor.matmul(acc[i % ACC], hid[a][:, par, k, P * B:P * B + P],
                                               down_w[b][:, k, HALF * h:HALF * h + HALF],
                                               start=(m == 0), stop=(m == 5))
                    ins.then_inc(acc_ready, 1)

            wait_evac(pe, ("mt", 7, 1))
            up(M4, NP0 + 4)
            up(M4 + 1, NP0 + 8)
            down(0, 0, M4 + 2, NP0 + 12)
            with pe.Fori(2, NJ, 2) as k:
                for par in range(2):
                    kk = k + par
                    up(M4 + 5 * kk - 4, NP0 + 8 * kk)
                    down(kk - 1, 1 - par, M4 + 5 * kk - 3, NP0 + 8 * kk + 4)
            down(NJ - 1, 1, M4 + 5 * NJ - 4, NP0 + 8 * NJ)


INPUTS = ("x", "c", "positions", "norm_g", "w_ada", "b_ada", "w_in", "conv_w", "conv_b", "conv_ln_g", "conv_ln_b",
          "w_conv_out", "w_att_out", "w_o", "final_g", "g_mix_pre_2", "w_in_2", "b_in_2", "w_pool_2",
          "pool_scale_2", "attn_sinks_2", "w_branch_pool_2", "w_branch_attn_2", "w_out_2", "g_mix_post_2",
          "g_mlp_pre_2", "w_up_2", "w_down_2", "g_mlp_post_2")


def kernel(**inputs):
    import concourse.bacc as bacc
    from concourse.bass_utils import run_bass_kernel_spmd

    nc = bacc.Bacc("TRN2", target_bir_lowering=False, num_devices=1)
    arrays, A = {}, {}
    laid_out = dict(inputs)
    columns = lambda a: np.asarray(a).reshape(-1, P).T
    for name in ("c", "norm_g", "conv_b", "conv_ln_g", "conv_ln_b", "pool_scale_2"):
        laid_out[name] = columns(inputs[name])
    laid_out["b_in_2_cols"] = columns(inputs["b_in_2"])
    laid_out["conv_w"] = np.asarray(inputs["conv_w"])[0].T
    pos = np.asarray(inputs["positions"])[0]
    laid_out["positions"] = np.concatenate(
        [pos.reshape(NB, P).T,
         pos.reshape(2, P, 4).transpose(1, 2, 0).reshape(P, 8),
         pos.reshape(P, 8)], axis=1)
    for name in INPUTS + ("b_in_2_cols",):
        a = np.ascontiguousarray(laid_out[name])
        arrays["in_" + name] = a
        A[name] = nc.dram_tensor("in_" + name, a.shape, mybir.dt.from_np(a.dtype), kind="ExternalInput").ap()
    out = nc.dram_tensor("out_y", (1, S, D), F32, kind="ExternalOutput").ap()
    build(nc, A, out[0])
    r = run_bass_kernel_spmd(nc, [arrays], core_ids=[0])
    return r.results[0]["out_y"]
```
